# Optimizing a Trainium2 kernel written in Bass

```python
import math
import jax
import jax.numpy as jnp
from jax import lax
import numpy as np

D_MODEL = 1024
BATCH = 1
SEQ = 256
DEPTH = 2

GRID_W = 64
CTX_LEN = 256
EPS = 1e-6
ROPE_BASE = 10000.0
QBLK = 128

HEAD_DIM = 64
SWA_HEADS = 4
SWA_KV_HEADS = 2
WINDOW = 128

DIFF_HEADS = 4
DIFF_QK_DIM = 32
DIFF_V_DIM = 64

MLA_HEADS = 4
MLA_Q_RANK = 192
MLA_KV_RANK = 128
MLA_NOPE = 64
MLA_ROPE = 32
MLA_V = 64

GDN_HEADS = 4
GDN_DK = 64
GDN_DV = 64
GDN_CONV = 5
GDN_CHUNK = 64
GDN_QKV = 2 * GDN_HEADS * GDN_DK + GDN_HEADS * GDN_DV

N_EXPERTS = 64
N_GROUPS = 8
TOPK_GROUPS = 4
TOP_K = 6
EXPERT_FF = 256
SHARED_FF = 256
ROUTED_SCALE = 2.5
MOE_BLOCK = 128

IN_SPLITS = (
    SWA_HEADS * HEAD_DIM,
    SWA_KV_HEADS * HEAD_DIM,
    SWA_KV_HEADS * HEAD_DIM,
    DIFF_HEADS * 2 * DIFF_QK_DIM,
    DIFF_HEADS * 2 * DIFF_QK_DIM,
    DIFF_HEADS * DIFF_V_DIM,
    MLA_Q_RANK,
    MLA_KV_RANK,
    MLA_ROPE,
    GDN_QKV,
    GDN_HEADS * GDN_DV,
    GDN_HEADS,
    GDN_HEADS,
    GDN_HEADS,
    GDN_HEADS,
)
IN_WIDTH = sum(IN_SPLITS)
MIX_WIDTH = SWA_HEADS * HEAD_DIM + DIFF_HEADS * DIFF_V_DIM + MLA_HEADS * MLA_V + GDN_HEADS * GDN_DV

kernel_name = 'hybrid_parallel_heads_moe_diffusion_block'

def rmsnorm(x, g):
    xf = x.astype(jnp.float32)
    y = xf * lax.rsqrt(jnp.mean(xf * xf, axis=-1, keepdims=True) + EPS)
    return (y * g.astype(jnp.float32)).astype(x.dtype)

def l2norm(x):
    xf = x.astype(jnp.float32)
    return (xf * lax.rsqrt(jnp.sum(xf * xf, axis=-1, keepdims=True) + EPS)).astype(x.dtype)

def axial_rope(rows, dim):
    quarter = dim // 4
    inv = ROPE_BASE ** (-jnp.arange(quarter, dtype=jnp.float32) / quarter)
    r = jnp.repeat(jnp.arange(rows, dtype=jnp.float32), GRID_W)
    col = jnp.tile(jnp.arange(GRID_W, dtype=jnp.float32), rows)
    ang = jnp.concatenate([r[:, None] * inv, col[:, None] * inv], axis=-1)
    return jnp.cos(ang), jnp.sin(ang)

def apply_rope(x, cos, sin):
    half = x.shape[-1] // 2
    shape = (x.shape[1],) + (1,) * (x.ndim - 3) + (half,)
    c = cos.reshape(shape).astype(x.dtype)
    s = sin.reshape(shape).astype(x.dtype)
    x1, x2 = x[..., :half], x[..., half:]
    return jnp.concatenate([x1 * c - x2 * s, x2 * c + x1 * s], axis=-1)

def sweep_query_blocks(fn, *qs):
    B, T = qs[0].shape[:2]
    nb = T // QBLK
    blocks = tuple(jnp.moveaxis(q.reshape((B, nb, QBLK) + q.shape[2:]), 1, 0) for q in qs)
    out = lax.map(lambda args: fn(*args), blocks)
    out = jnp.moveaxis(out, 0, 1)
    return out.reshape((B, T) + out.shape[3:])

def swa_attention(q, k, v, qc, kc, vc, sinks, need_ctx):
    B, S = q.shape[:2]
    C = kc.shape[1]
    G = SWA_HEADS // SWA_KV_HEADS
    nb = S // WINDOW
    scale = HEAD_DIM ** -0.5
    sink = sinks.astype(jnp.float32).reshape(SWA_KV_HEADS, G)[:, :, None, None]

    def band(t):
        tb = jnp.pad(t, ((0, 0), (WINDOW, WINDOW), (0, 0), (0, 0))).reshape(B, nb + 2, WINDOW, SWA_KV_HEADS, HEAD_DIM)
        return jnp.concatenate([tb[:, :-2], tb[:, 1:-1], tb[:, 2:]], axis=2)

    kw, vw = band(k), band(v)
    qb = q.reshape(B, nb, WINDOW, SWA_KV_HEADS, G, HEAD_DIM)
    qpos = jnp.arange(nb)[:, None] * WINDOW + jnp.arange(WINDOW)[None, :]
    kpos = jnp.arange(nb)[:, None] * WINDOW - WINDOW + jnp.arange(3 * WINDOW)[None, :]
    kp = kpos[:, None, :]
    valid = (jnp.abs(kp - qpos[:, :, None]) <= WINDOW) & (kp >= 0) & (kp < S)
    s_loc = jnp.einsum('bnqhgd,bnkhd->bnhgqk', qb, kw).astype(jnp.float32) * scale
    s_loc = jnp.where(valid[None, :, None, None], s_loc, -jnp.inf)
    s_ctx = jnp.einsum('bnqhgd,bkhd->bnhgqk', qb, kc).astype(jnp.float32) * scale
    s_sink = jnp.broadcast_to(sink, s_loc.shape[:-1] + (1,))
    p = jax.nn.softmax(jnp.concatenate([s_loc, s_ctx, s_sink], axis=-1), axis=-1)
    L = 3 * WINDOW
    p_loc = p[..., :L].astype(v.dtype)
    p_ctx = p[..., L:L + C].astype(v.dtype)
    o = jnp.einsum('bnhgqk,bnkhd->bnqhgd', p_loc, vw) + jnp.einsum('bnhgqk,bkhd->bnqhgd', p_ctx, vc)
    y = o.reshape(B, S, SWA_HEADS * HEAD_DIM)
    yc = None
    if need_ctx:
        qcg = qc.reshape(B, C, SWA_KV_HEADS, G, HEAD_DIM)
        s = jnp.einsum('bqhgd,bkhd->bhgqk', qcg, kc).astype(jnp.float32) * scale
        s = jnp.concatenate([s, jnp.broadcast_to(sink, s.shape[:-1] + (1,))], axis=-1)
        pc = jax.nn.softmax(s, axis=-1)[..., :C].astype(vc.dtype)
        yc = jnp.einsum('bhgqk,bkhd->bqhgd', pc, vc).reshape(B, C, SWA_HEADS * HEAD_DIM)
    return y, yc

def diff_attention(q, k, v, qc, kc, vc, lam, lam_init, norm_g, need_ctx):
    scale = DIFF_QK_DIM ** -0.5

    def make(keys, vals):
        def fn(qb):
            s = jnp.einsum('bqhmd,bkhmd->bhmqk', qb, keys).astype(jnp.float32) * scale
            p = jax.nn.softmax(s, axis=-1)
            p = (p[:, :, 0] - lam * p[:, :, 1]).astype(vals.dtype)
            return jnp.einsum('bhqk,bkhd->bqhd', p, vals)
        return fn

    def finish(o):
        o = rmsnorm(o, norm_g) * (1.0 - lam_init)
        return o.reshape(o.shape[:2] + (-1,))

    y = finish(sweep_query_blocks(make(jnp.concatenate([k, kc], axis=1), jnp.concatenate([v, vc], axis=1)), q))
    yc = finish(sweep_query_blocks(make(kc, vc), qc)) if need_ctx else None
    return y, yc

def mla_attention(cq, ckv, kr, cq_c, ckv_c, kr_c, gq, gkv, w_uq, w_ukv, rope, need_ctx):
    scale = (MLA_NOPE + MLA_ROPE) ** -0.5

    def queries(cq_, rotate):
        q = (rmsnorm(cq_, gq) @ w_uq).reshape(cq_.shape[:2] + (MLA_HEADS, MLA_NOPE + MLA_ROPE))
        qr = q[..., MLA_NOPE:]
        return q[..., :MLA_NOPE], (apply_rope(qr, *rope) if rotate else qr)

    def keys_values(ckv_, kr_, rotate):
        kv = (rmsnorm(ckv_, gkv) @ w_ukv).reshape(ckv_.shape[:2] + (MLA_HEADS, MLA_NOPE + MLA_V))
        return kv[..., :MLA_NOPE], (apply_rope(kr_, *rope) if rotate else kr_), kv[..., MLA_NOPE:]

    def make(kn_, kr_, v_):
        def fn(qn_b, qr_b):
            s = jnp.einsum('bqhd,bkhd->bhqk', qn_b, kn_) + jnp.einsum('bqhr,bkr->bhqk', qr_b, kr_)
            p = jax.nn.softmax(s.astype(jnp.float32) * scale, axis=-1).astype(v_.dtype)
            return jnp.einsum('bhqk,bkhd->bqhd', p, v_)
        return fn

    kn, krl, v = keys_values(ckv, kr, True)
    kn_c, krc, v_c = keys_values(ckv_c, kr_c, False)
    qn, qr = queries(cq, True)
    y = sweep_query_blocks(make(jnp.concatenate([kn, kn_c], axis=1), jnp.concatenate([krl, krc], axis=1),
                                jnp.concatenate([v, v_c], axis=1)), qn, qr)
    y = y.reshape(y.shape[:2] + (-1,))
    yc = None
    if need_ctx:
        qn_c, qr_c = queries(cq_c, False)
        yc = sweep_query_blocks(make(kn_c, krc, v_c), qn_c, qr_c)
        yc = yc.reshape(yc.shape[:2] + (-1,))
    return y, yc

def short_conv(x, w):
    pad = GDN_CONV // 2
    y = lax.conv_general_dilated(x, w[:, None, :].astype(x.dtype), window_strides=(1,), padding=[(pad, pad)],
                                 dimension_numbers=('NWC', 'WIO', 'NWC'), feature_group_count=x.shape[-1])
    return jax.nn.silu(y)

def gated_delta_chunked(q, k, v, g, beta, state):
    B, T, H, _ = q.shape
    dv = v.shape[-1]
    n = T // GDN_CHUNK
    Cc = GDN_CHUNK

    def to_chunks(t):
        t = jnp.moveaxis(t.astype(jnp.float32), 2, 1)
        return t.reshape((B, H, n, Cc) + t.shape[3:])

    qf, kf, vf = to_chunks(q), to_chunks(k), to_chunks(v)
    gc = jnp.cumsum(to_chunks(g), axis=-1)
    bt = to_chunks(beta)
    kb = kf * bt[..., None]
    vb = vf * bt[..., None]
    tri_incl = jnp.tril(jnp.ones((Cc, Cc), bool))
    tri_strict = jnp.tril(jnp.ones((Cc, Cc), bool), -1)
    diff = gc[..., :, None] - gc[..., None, :]
    decay = jnp.where(tri_incl, jnp.exp(jnp.where(tri_incl, diff, 0.0)), 0.0)
    a_mat = jnp.where(tri_strict, jnp.einsum('bhnid,bhnjd->bhnij', kb, kf) * decay, 0.0)
    eye = jnp.eye(Cc, dtype=jnp.float32)
    tmat = lax.linalg.triangular_solve(a_mat + eye, jnp.broadcast_to(eye, a_mat.shape), left_side=True, lower=True)
    eg = jnp.exp(gc)[..., None]
    u = tmat @ vb
    w = tmat @ (kb * eg)
    attn = jnp.einsum('bhnid,bhnjd->bhnij', qf, kf) * decay
    qg = qf * eg
    glast = gc[..., -1]
    kdec = kf * jnp.exp(glast[..., None] - gc)[..., None]

    def step(S, xs):
        qg_i, w_i, u_i, at_i, kd_i, gl_i = xs
        v_new = u_i - jnp.einsum('bhcd,bhde->bhce', w_i, S)
        o = jnp.einsum('bhcd,bhde->bhce', qg_i, S) + jnp.einsum('bhij,bhje->bhie', at_i, v_new)
        S = S * jnp.exp(gl_i)[..., None, None] + jnp.einsum('bhcd,bhce->bhde', kd_i, v_new)
        return S, o

    xs = tuple(jnp.moveaxis(t, 2, 0) for t in (qg, w, u, attn, kdec, glast))
    S, o = lax.scan(step, state, xs)
    o = jnp.moveaxis(jnp.moveaxis(o, 0, 2).reshape(B, H, T, dv), 1, 2)
    return o.astype(v.dtype), S

def gdn_mixer(qkv, z, af, ab, bf, bb, qkv_c, z_c, af_c, ab_c, bf_c, bb_c,
              conv_w, a_log_f, a_log_b, dtb_f, dtb_b, norm_g, need_ctx):
    f32 = jnp.float32

    def prep(qkv_, af_, ab_, bf_, bb_):
        B, T = qkv_.shape[:2]
        hcv = short_conv(qkv_, conv_w)
        q, k, v = jnp.split(hcv, [GDN_HEADS * GDN_DK, 2 * GDN_HEADS * GDN_DK], axis=-1)
        q = l2norm(q.reshape(B, T, GDN_HEADS, GDN_DK)) * (GDN_DK ** -0.5)
        k = l2norm(k.reshape(B, T, GDN_HEADS, GDN_DK))
        v = v.reshape(B, T, GDN_HEADS, GDN_DV)
        g_f = -jnp.exp(a_log_f.astype(f32)) * jax.nn.softplus(af_.astype(f32) + dtb_f.astype(f32))
        g_b = -jnp.exp(a_log_b.astype(f32)) * jax.nn.softplus(ab_.astype(f32) + dtb_b.astype(f32))
        return q, k, v, g_f, jax.nn.sigmoid(bf_.astype(f32)), g_b, jax.nn.sigmoid(bb_.astype(f32))

    q, k, v, gf, btf, gb, btb = prep(qkv, af, ab, bf, bb)
    qc, kc, vc, gfc, btfc, gbc, btbc = prep(qkv_c, af_c, ab_c, bf_c, bb_c)
    s0 = jnp.zeros((q.shape[0], GDN_HEADS, GDN_DK, GDN_DV), f32)
    flip = lambda t: jnp.flip(t, axis=1)
    oc_f, s_cf = gated_delta_chunked(qc, kc, vc, gfc, btfc, s0)
    oc_b, s_cb = gated_delta_chunked(flip(qc), flip(kc), flip(vc), flip(gbc), flip(btbc), s0)
    o_f, _ = gated_delta_chunked(q, k, v, gf, btf, s_cf)
    o_b, _ = gated_delta_chunked(flip(q), flip(k), flip(v), flip(gb), flip(btb), s_cb)

    def gated_out(o, zz):
        B, T = zz.shape[:2]
        o = rmsnorm(o, norm_g) * jax.nn.silu(zz.reshape(B, T, GDN_HEADS, GDN_DV))
        return o.reshape(B, T, GDN_HEADS * GDN_DV)

    y = gated_out(o_f + flip(o_b), z)
    yc = gated_out(oc_f + flip(oc_b), z_c) if need_ctx else None
    return y, yc

def moe_ffn(x2, w_router, bias, w_gate, w_up, w_down, sw_gate, sw_up, sw_down):
    T, D = x2.shape
    f32 = jnp.float32
    scores = jax.nn.sigmoid(x2.astype(f32) @ w_router.astype(f32))
    choice = scores + bias.astype(f32)
    per_group = N_EXPERTS // N_GROUPS
    grp_score = lax.top_k(choice.reshape(T, N_GROUPS, per_group), 2)[0].sum(-1)
    _, top_g = lax.top_k(grp_score, TOPK_GROUPS)
    gmask = jnp.any(top_g[:, :, None] == jnp.arange(N_GROUPS)[None, None, :], axis=1)
    emask = jnp.repeat(gmask, per_group, axis=1)
    _, idx = lax.top_k(jnp.where(emask, choice, -jnp.inf), TOP_K)
    wts = jnp.take_along_axis(scores, idx, axis=-1)
    wts = wts / jnp.sum(wts, axis=-1, keepdims=True) * ROUTED_SCALE

    A = T * TOP_K
    flat_e = idx.reshape(-1)
    flat_t = jnp.repeat(jnp.arange(T, dtype=jnp.int32), TOP_K)
    flat_w = wts.reshape(-1)
    order = jnp.argsort(flat_e)
    se, st, sw = flat_e[order], flat_t[order], flat_w[order]
    counts = jnp.zeros((N_EXPERTS,), jnp.int32).at[flat_e].add(1)
    start = jnp.cumsum(counts) - counts
    padded = (counts + MOE_BLOCK - 1) // MOE_BLOCK * MOE_BLOCK
    pad_end = jnp.cumsum(padded)
    pad_start = pad_end - padded
    dest = pad_start[se] + (jnp.arange(A, dtype=jnp.int32) - start[se])
    n_blocks = -(-(A + N_EXPERTS * (MOE_BLOCK - 1)) // MOE_BLOCK)
    buf_t = jnp.full((n_blocks * MOE_BLOCK,), T, jnp.int32).at[dest].set(st)
    buf_w = jnp.zeros((n_blocks * MOE_BLOCK,), f32).at[dest].set(sw)
    blk_e = jnp.minimum(jnp.searchsorted(pad_end, jnp.arange(n_blocks, dtype=jnp.int32) * MOE_BLOCK, side='right'),
                        N_EXPERTS - 1)
    xpad = jnp.concatenate([x2, jnp.zeros((1, D), x2.dtype)], axis=0)

    def body(y, blk):
        t_idx, wb, e = blk
        xb = xpad[t_idx]
        hb = jax.nn.silu(xb @ w_gate[e]) * (xb @ w_up[e])
        yb = (hb @ w_down[e]).astype(f32) * wb[:, None]
        return y.at[t_idx].add(yb), None

    y, _ = lax.scan(body, jnp.zeros((T + 1, D), f32),
                    (buf_t.reshape(n_blocks, MOE_BLOCK), buf_w.reshape(n_blocks, MOE_BLOCK), blk_e))
    shared = (jax.nn.silu(x2 @ sw_gate) * (x2 @ sw_up)) @ sw_down
    return y[:T].astype(x2.dtype) + shared

def mix_tokens(h, hc, rope_a, rope_b, rope_c, lam_init, w_in, w_out, sinks, lq1, lk1, lq2, lk2, diff_g,
               mla_gq, mla_gkv, w_uq, w_ukv, conv_w, a_log_f, a_log_b, dtb_f, dtb_b, gdn_g, need_ctx):
    f32 = jnp.float32
    cuts = [int(i) for i in np.cumsum(IN_SPLITS)[:-1]]
    (aq, ak, av, bq, bk, bv, cq, ckv, kr, dqkv, dz, daf, dab, dbf, dbb) = jnp.split(h @ w_in, cuts, axis=-1)
    (aq_c, ak_c, av_c, bq_c, bk_c, bv_c, cq_c, ckv_c, kr_c, dqkv_c, dz_c, daf_c, dab_c, dbf_c, dbb_c) = \
        jnp.split(hc @ w_in, cuts, axis=-1)
    heads = lambda t, *hs: t.reshape(t.shape[:2] + hs)

    y_a, yc_a = swa_attention(
        apply_rope(heads(aq, SWA_HEADS, HEAD_DIM), *rope_a),
        apply_rope(heads(ak, SWA_KV_HEADS, HEAD_DIM), *rope_a),
        heads(av, SWA_KV_HEADS, HEAD_DIM),
        heads(aq_c, SWA_HEADS, HEAD_DIM), heads(ak_c, SWA_KV_HEADS, HEAD_DIM), heads(av_c, SWA_KV_HEADS, HEAD_DIM),
        sinks, need_ctx)

    lam = (jnp.exp(jnp.sum(lq1.astype(f32) * lk1.astype(f32)))
           - jnp.exp(jnp.sum(lq2.astype(f32) * lk2.astype(f32))) + lam_init)
    y_b, yc_b = diff_attention(
        apply_rope(heads(bq, DIFF_HEADS, 2, DIFF_QK_DIM), *rope_b),
        apply_rope(heads(bk, DIFF_HEADS, 2, DIFF_QK_DIM), *rope_b),
        heads(bv, DIFF_HEADS, DIFF_V_DIM),
        heads(bq_c, DIFF_HEADS, 2, DIFF_QK_DIM), heads(bk_c, DIFF_HEADS, 2, DIFF_QK_DIM),
        heads(bv_c, DIFF_HEADS, DIFF_V_DIM), lam, lam_init, diff_g, need_ctx)

    y_c, yc_c = mla_attention(cq, ckv, kr, cq_c, ckv_c, kr_c, mla_gq, mla_gkv, w_uq, w_ukv, rope_c, need_ctx)

    y_d, yc_d = gdn_mixer(dqkv, dz, daf, dab, dbf, dbb, dqkv_c, dz_c, daf_c, dab_c, dbf_c, dbb_c,
                          conv_w, a_log_f, a_log_b, dtb_f, dtb_b, gdn_g, need_ctx)

    y = jnp.concatenate([y_a, y_b, y_c, y_d], axis=-1) @ w_out
    yc = (jnp.concatenate([yc_a, yc_b, yc_c, yc_d], axis=-1) @ w_out) if need_ctx else None
    return y, yc

def setup_inputs(seed: int = 0) -> dict:
    key = jax.random.key(seed)
    keys = iter(jax.random.split(key, 48))
    f32 = jnp.float32
    L, D = DEPTH, D_MODEL

    def normal(shape, scale):
        return jax.random.normal(next(keys), shape, f32) * scale

    def gain(shape):
        return 1.0 + 0.02 * jax.random.normal(next(keys), shape, f32)

    dt = jnp.exp(jax.random.uniform(next(keys), (L, 2, GDN_HEADS), f32, math.log(1e-3), math.log(1e-1)))
    dt_bias = dt + jnp.log(-jnp.expm1(-dt))
    a_log = jnp.log(jax.random.uniform(next(keys), (L, 2, GDN_HEADS), f32, 1.0, 16.0))
    return {
        'x': normal((BATCH, SEQ, D), 1.0),
        'c': normal((BATCH, D), 1.0),
        'ctx': normal((BATCH, CTX_LEN, D), 1.0),
        'c_ctx': normal((D,), 1.0),
        'w_ada': normal((L, D, 6 * D), 0.5 * D ** -0.5),
        'b_ada': normal((L, 6 * D), 0.01),
        'norm1_g': gain((L, D)),
        'norm2_g': gain((L, D)),
        'w_in': normal((L, D, IN_WIDTH), D ** -0.5),
        'w_out': normal((L, MIX_WIDTH, D), MIX_WIDTH ** -0.5),
        'swa_sinks': normal((L, SWA_HEADS), 0.5),
        'diff_lq1': normal((L, DIFF_QK_DIM), 0.1),
        'diff_lk1': normal((L, DIFF_QK_DIM), 0.1),
        'diff_lq2': normal((L, DIFF_QK_DIM), 0.1),
        'diff_lk2': normal((L, DIFF_QK_DIM), 0.1),
        'diff_norm_g': gain((L, DIFF_V_DIM)),
        'mla_q_norm_g': gain((L, MLA_Q_RANK)),
        'mla_kv_norm_g': gain((L, MLA_KV_RANK)),
        'mla_w_uq': normal((L, MLA_Q_RANK, MLA_HEADS * (MLA_NOPE + MLA_ROPE)), MLA_Q_RANK ** -0.5),
        'mla_w_ukv': normal((L, MLA_KV_RANK, MLA_HEADS * (MLA_NOPE + MLA_V)), MLA_KV_RANK ** -0.5),
        'gdn_conv_w': normal((L, GDN_CONV, GDN_QKV), GDN_CONV ** -0.5),
        'gdn_a_log_f': a_log[:, 0],
        'gdn_a_log_b': a_log[:, 1],
        'gdn_dt_bias_f': dt_bias[:, 0],
        'gdn_dt_bias_b': dt_bias[:, 1],
        'gdn_norm_g': gain((L, GDN_DV)),
        'moe_w_router': normal((L, D, N_EXPERTS), D ** -0.5),
        'moe_bias': normal((L, N_EXPERTS), 0.01),
        'moe_w_gate': normal((L, N_EXPERTS, D, EXPERT_FF), D ** -0.5),
        'moe_w_up': normal((L, N_EXPERTS, D, EXPERT_FF), D ** -0.5),
        'moe_w_down': normal((L, N_EXPERTS, EXPERT_FF, D), EXPERT_FF ** -0.5),
        'shared_w_gate': normal((L, D, SHARED_FF), D ** -0.5),
        'shared_w_up': normal((L, D, SHARED_FF), D ** -0.5),
        'shared_w_down': normal((L, SHARED_FF, D), SHARED_FF ** -0.5),
        'final_norm_g': gain((D,)),
    }

def reference(x, c, ctx, c_ctx, w_ada, b_ada, norm1_g, norm2_g, w_in, w_out, swa_sinks,
              diff_lq1, diff_lk1, diff_lq2, diff_lk2, diff_norm_g, mla_q_norm_g, mla_kv_norm_g,
              mla_w_uq, mla_w_ukv, gdn_conv_w, gdn_a_log_f, gdn_a_log_b, gdn_dt_bias_f, gdn_dt_bias_b,
              gdn_norm_g, moe_w_router, moe_bias, moe_w_gate, moe_w_up, moe_w_down,
              shared_w_gate, shared_w_up, shared_w_down, final_norm_g):
    B, S, D = x.shape
    rows = S // GRID_W
    rope_a = axial_rope(rows, HEAD_DIM)
    rope_b = axial_rope(rows, DIFF_QK_DIM)
    rope_c = axial_rope(rows, MLA_ROPE)
    s_lat = jax.nn.silu(c)
    s_ctx = jax.nn.silu(c_ctx)
    xc = ctx
    for l in range(DEPTH):
        last = l == DEPTH - 1
        lam_init = 0.8 - 0.6 * math.exp(-0.3 * l)
        mod = (s_lat @ w_ada[l] + b_ada[l]).reshape(B, 6, 1, D)
        modc = (s_ctx @ w_ada[l] + b_ada[l]).reshape(6, D)
        h = rmsnorm(x, norm1_g[l]) * (1.0 + mod[:, 1]) + mod[:, 0]
        hc = rmsnorm(xc, norm1_g[l]) * (1.0 + modc[1]) + modc[0]
        y, yc = mix_tokens(h, hc, rope_a, rope_b, rope_c, lam_init, w_in[l], w_out[l], swa_sinks[l],
                           diff_lq1[l], diff_lk1[l], diff_lq2[l], diff_lk2[l], diff_norm_g[l],
                           mla_q_norm_g[l], mla_kv_norm_g[l], mla_w_uq[l], mla_w_ukv[l],
                           gdn_conv_w[l], gdn_a_log_f[l], gdn_a_log_b[l], gdn_dt_bias_f[l], gdn_dt_bias_b[l],
                           gdn_norm_g[l], not last)
        x = x + mod[:, 2] * y
        h = rmsnorm(x, norm2_g[l]) * (1.0 + mod[:, 4]) + mod[:, 3]
        moe_args = (moe_w_router[l], moe_bias[l], moe_w_gate[l], moe_w_up[l], moe_w_down[l],
                    shared_w_gate[l], shared_w_up[l], shared_w_down[l])
        if last:
            f = moe_ffn(h.reshape(B * S, D), *moe_args).reshape(B, S, D)
        else:
            xc = xc + modc[2] * yc
            hc = rmsnorm(xc, norm2_g[l]) * (1.0 + modc[4]) + modc[3]
            f_all = moe_ffn(jnp.concatenate([h.reshape(B * S, D), hc.reshape(-1, D)], axis=0), *moe_args)
            f = f_all[:B * S].reshape(B, S, D)
            xc = xc + modc[5] * f_all[B * S:].reshape(xc.shape)
        x = x + mod[:, 5] * f
    return rmsnorm(x, final_norm_g)


_drawn_inputs = setup_inputs


def setup_inputs(seed=0):
    import zlib

    import numpy as np

    out = dict(_drawn_inputs(seed))
    spreads = {}
    factors = {'swa_sinks': 8.0,
     'diff_norm_g': 2.922,
     'mla_q_norm_g': 5.52,
     'mla_kv_norm_g': 5.163,
     'gdn_norm_g': 2.909,
     'final_norm_g': 2.75}
    for name, (base, spread) in spreads.items():
        noise = np.random.default_rng([zlib.crc32(name.encode()), seed]).standard_normal(out[name].shape)
        drawn = base * np.exp(spread * noise) if base else spread * noise
        out[name] = jnp.asarray(drawn.astype(out[name].dtype))
    for name, factor in factors.items():
        out[name] = (out[name] * factor).astype(out[name].dtype)
    return out
```

```python
from contextlib import ExitStack
import math

import numpy as np

import concourse.bass as bass
from concourse import mybir
from concourse.alu_op_type import AluOpType as ALU

ACT = mybir.ActivationFunctionType
AX = mybir.AxisListType
F32 = mybir.dt.float32
I32 = mybir.dt.int32

P = 128
D, KD = 1024, 1024 // P
SEQ = 256
T, NT, NLAT = 512, 4, 2
DEPTH = 2
IN_W = 2672
EPS = 1e-6
NE, TOPK, NG, TOPG = 64, 6, 8, 4
FF = 256
RING = 3
SLOT = KD * 768
CAP = P
CODES = 8 * T

CO, _n = {}, 0
for _name, _w in (('ident', P), ('ones', P), ('le', P), ('ge', P), ('big_f', P), ('big_b', P),
                  ('in_f', P), ('in_b', P), ('off_f', P), ('off_b', P), ('swa', 2 * T),
                  ('cos_a', 2 * 64), ('sin_a', 2 * 64), ('cos_b', 2 * 32), ('sin_b', 2 * 32),
                  ('experts', NE), ('codes', NT * TOPK), ('eps', 1)):
    CO[_name] = (_n, _n + _w)
    _n += _w
NC = _n


def constants():
    c = np.zeros((P, NC), np.float32)
    p, f = np.arange(P)[:, None], np.arange(P)[None, :]

    def put(name, a):
        c[:, CO[name][0]:CO[name][1]] = np.asarray(a, np.float32).reshape(P, -1)

    put('ident', p == f)
    put('ones', np.ones((P, P)))
    put('le', p <= f)
    put('ge', p >= f)
    put('big_f', np.where(p >= f, 0, 1e30))
    put('big_b', np.where(p <= f, 0, 1e30))
    same = p // 16 == f // 16
    put('in_f', (p > f) & same)
    put('in_b', (p < f) & same)
    put('off_f', (p > f) & ~same)
    put('off_b', (p < f) & ~same)
    mask = np.zeros((P, 2, T))
    for i in range(2):
        q = i * P + np.arange(P)[:, None]
        mask[:, i, :SEQ] = np.where(np.abs(np.arange(SEQ)[None] - q) <= 128, 0, -1e30)
    put('swa', mask)
    t = np.arange(SEQ)
    for name, dim in (('a', 64), ('b', 32)):
        quarter = dim // 4
        inv = np.float32(10000.0) ** (-np.arange(quarter, dtype=np.float32) / np.float32(quarter))
        ang = np.concatenate([(t // 64).astype(np.float32)[:, None] * inv, (t % 64).astype(np.float32)[:, None] * inv], 1)
        cos, sin = np.cos(ang), np.sin(ang)
        put('cos_' + name, np.concatenate([cos, cos], 1).reshape(2, P, dim).transpose(1, 0, 2))
        put('sin_' + name, np.concatenate([-sin, sin], 1).reshape(2, P, dim).transpose(1, 0, 2))
    put('experts', np.broadcast_to(np.arange(NE), (P, NE)))
    token = np.arange(NT)[None, :, None] * P + np.arange(P)[:, None, None]
    put('codes', CODES - 8 * token - np.arange(TOPK)[None, None, :])
    put('eps', np.full((P, 1), EPS))
    return c


PHASE = {'lam': 'mod', 'rope': 'proj', 'lat': 'proj', 'tr': 'turn', 'up': 'turn', 'tm': 'turn', 'kf': 'turn', 'pad': 'turn',
         'dif': 'att', 'conv': 'gdn', 'gate': 'gdn', 'qk': 'gdn', 'gt': 'gdn', 'gq': 'gdn', 'gc': 'gdn',
         'yt': 'out', 'rt': 'moe', 'sh': 'moe', 'xg': 'moe', 'gout': 'heads', 'gdn': 'heads'}


class Steps:

    def __init__(self, nc, ctx, known):
        self.nc, self.ctx, self.known, self.seen, self.count, self.sems = nc, ctx, known, {}, {}, {}

    def sem(self, name):
        if name not in self.sems:
            self.sems[name] = self.ctx.enter_context(self.nc.semaphore(name))
        return self.sems[name]

    @staticmethod
    def name(engine, step, layer):
        phase = step.split('.')[0]
        return f"{engine}_{phase if engine == 'DMA' else PHASE.get(phase, phase)}_{layer}"

    def done(self, engine, step, layer, *at, by=1):
        name = self.name(engine, step, layer)
        self.count[name] = self.count.get(name, 0) + by
        key = (engine, step, layer, *at)
        assert key not in self.seen, key
        self.seen[key] = self.count[name]
        return self.sem(name), by

    def after(self, engine, step, layer, *at):
        name = self.name(engine, step, layer)
        value = self.known[(engine, step, layer, *at)] if self.known else 1
        return self.sem(name), value


def ring_chunks(l):
    return ([('ada', j) for j in range(8)] + [('in', j) for j in range(4)] + [('mla', 0)]
            + [('out', j) for j in range(2)] + [('router', 0), ('shared', 0)] + [('expert', e) for e in range(NE)])


PER_LAYER = len(ring_chunks(0))
CHUNK = {kind: i for i, kind in reversed(list(enumerate(ring_chunks(0))))}


def build(nc, io, out, known):
    with ExitStack() as ctx:
        st = Steps(nc, ctx, known)
        done, after = st.done, st.after

        def sb(name, n, parts=P, dt=F32):
            return ctx.enter_context(nc.sbuf_tensor(name, [parts, n], dt))

        h2_rows = nc.dram_tensor('h2_rows', (T, D), F32).ap()
        y_rows = nc.dram_tensor('y_rows', (CODES, D), F32).ap()

        cst = sb('cst', NC)
        ring = sb('ring', RING * SLOT)
        x_t = sb('x_t', KD * T)
        h_t = sb('h_t', KD * T)
        rows = [sb(f'rows{l}', P) for l in range(DEPTH)]
        cols = [sb(f'cols{l}', 118) for l in range(DEPTH)]
        BCW = 192 + 128 + 64 + 64 + 4 + 64 + 128 + 16
        bc = [sb(f'bc{l}', BCW) for l in range(DEPTH)]
        mod = [sb(f'mod{l}', 96) for l in range(DEPTH)]
        amp = [sb(f'amp{l}', 32) for l in range(DEPTH)]
        small = sb('small', 96)
        flags = sb('flags', DEPTH, dt=I32)
        ARENA = 21400
        arena = sb('arena', ARENA)
        bank = [ctx.enter_context(nc.psum_tensor(f'bank{b}', [P, 512], F32)) for b in range(8)]

        def C(name):
            return cst[:, CO[name][0]:CO[name][1]]

        def area(at, *dims, parts=P, dt=None):
            n = int(np.prod(dims))
            assert at + n <= ARENA, (at, n)
            v = arena[0:parts, at:at + n]
            if dt is not None:
                v = v.bitcast(dt)
            if len(dims) == 2:
                v = v.rearrange("p (a b) -> p a b", b=dims[1])
            if len(dims) == 3:
                v = v.rearrange("p (a b c) -> p a b c", b=dims[1], c=dims[2])
            return v, at + n

        ident, ones = C('ident'), C('ones')
        xT = x_t[:].rearrange("p (c t) -> p c t", t=T)
        hT = h_t[:].rearrange("p (c t) -> p c t", t=T)
        Y = h_t[:].rearrange("p (i n) -> p i n", n=D)
        SC = small[:, 0:16].rearrange("p (k g) -> p k g", g=2)
        lamt = small[:, 16:24]
        GNS = small[:, 64:80]
        NEXP = small[:, 80:88]

        DZ, at = area(0, NT, 272)
        GP, at_gdn = area(at, 6, 520)
        x_rows, _ = area(at_gdn, NT, D)
        AV, at = area(at_gdn, NT, 128)
        BV, at = area(at, NT, 256)
        QMT, at_pa = area(at, 4, T, parts=96)
        CC, _ = area(at, NT, 352)
        rstd_s, n_at = area(at, T)
        rstd_t, n_at = area(n_at, T)
        PA, at_pb = area(at_pa, NT, 384)
        QM, _ = area(at_pa, NT, 384)
        PX, _ = area(at_pa, 3, 512)
        PB, at_qa = area(at_pb, NT, 512)
        KMT, _ = area(at_pb, 4, T, parts=96)
        DD, _ = area(at_pb, NT, 8, 64)
        QAT, at = area(at_qa, 2, T)
        KAT, at = area(at, T)
        DQT, at = area(at, 2, T)
        tA, t_at = area(at_qa, 1024)
        tB, t_at = area(t_at, 1024)
        DSQ, t_at = area(at_qa, NT * 4, 64)
        DS2, t_at = area(t_at, NT * 4, 64)
        DKT, at = area(at, 2, T)
        CQT0, _ = area(at, 512)
        CQT, at = area(at, 2, T, parts=96)
        CKT, at = area(at, T)
        KV, at = area(at, NT, 512)
        at_kf = at
        KF, at = area(at_kf, NT * 4, 96)
        PXT, _ = area(at_kf, 3, 512)
        SM, at = area(at, 512)
        NEGM, at = area(at, NT, 16)
        SUMS, at = area(at, NT, 16)
        RINV, at = area(at, NT, 16)
        ESINK, at = area(at, NT, 4)
        SST, at = area(at, NT, 4)

        GT, _ = area(NT * 272, NT, 768)
        CV, at = area(at_gdn, 6, T)
        GQ, at = area(at, NT, 512, parts=64)
        GK, at = area(at, NT, 512, parts=64)
        GA, at = area(at, NT, 8)
        GG, at = area(at, NT, 8)
        GB, at = area(at, NT, 8)
        GC, at = area(at, NT, 8)
        GN, at = area(at, NT, 8)
        GW, at_w = area(at, NT * 8)
        QSQ, _ = area(at_w, NT * 8, 64)
        GSQ, _ = area(at_w, NT * 4, 64)
        blocks = [arena[:, q:q + 512] for q in list(range(at_gdn, at_gdn + 3072 - 511, 512)) + list(range(at_w, ARENA - 511, 512))]
        blocks += [ring[:, q:q + 512] for q in range(2 * SLOT, 3 * SLOT, 512)]
        W = []
        for d in range(2):
            w = {n: blocks.pop() for n in ('cum', 'dec', 'kd', 'b', 'bt', 'z', 'n', 'b2', 'b2t', 'b4', 'b4t',
                                           'att', 'attt', 'r', 'qgt')}
            for n in (('qg', 'kdec'), ('vnew', 'u'), ('s', 'stmp')):
                v = blocks.pop()
                w[n[0]], w[n[1]] = v[:, 0:256], v[:, 256:512]
            w['m'], w['mt'], w['m2'], w['m2t'], w['m4t'], w['imt'] = w['b'], w['bt'], w['b2'], w['b2t'], w['b4'], w['b4t']
            w['b8'], w['x0'], w['x1'], w['x2'] = w['cum'], w['kd'], w['dec'], w['kd']
            w['wt'] = w['r']
            w['egl'], w['eg'], w['ekd'], w['beg'] = (small[:, 32 + 16 * d + 4 * k:36 + 16 * d + 4 * k] for k in range(4))
            W.append(w)

        YT, _ = area(at_gdn, KD, T)

        rstd2_s, at = area(0, T)
        rstd2_t, at = area(at, T)
        LG, at = area(at, NT, 64)
        CH, at = area(at, NT, 64)
        TOP8, at = area(at, NT * 8, 8)
        GSC, at = area(at, NT, 8)
        GT8, at = area(at, NT, 8)
        GIX, at = area(at, NT, 8, dt=I32)
        GIF, at = area(at, NT, 8)
        GMK, at = area(at, NT, 8)
        OHG, at = area(at, NT * 4, 8)
        E8, at = area(at, NT, 8)
        EIX, at = area(at, NT, 8, dt=I32)
        EIF, at = area(at, NT, 8)
        OH, at = area(at, NT * 6, 64)
        OH2, at = area(at, NT * 6, 64)
        WK, at = area(at, NT, 6)
        WS, at = area(at, NT)
        VC, at = area(at, NT, 64)
        VT, at = (arena[0:NE, at:at + T], at + T)
        LST, at = (arena[0:NE, at:at + T], at + T)
        LEFT, at = area(at, 1)
        COLS = NE * (T // CAP)
        CODI, at = (arena[:, at:at + COLS].bitcast(I32), at + COLS)
        TOKI, at = (arena[:, at:at + COLS].bitcast(I32), at + COLS)
        cix, at = (arena[:, at:at + 3].bitcast(I32), at + 3)
        tix, at = (arena[:, at:at + 3].bitcast(I32), at + 3)
        at_sh = at
        HR, _ = area(at, NT // 2, D)
        xg, at = area(at, 3, D)
        xgT, at = area(at, 3, D)
        sg, at = area(at, 3, FF)
        hh, at = area(at, 3, FF)
        hhT, at = area(at, 3, FF)
        yy, at = area(at, 3, D)
        SH1, _ = area(at, 2, T)
        SH2, _ = area(at + 2 * T, 2, T)
        YR, at = area(at_sh, 6, D)
        YC, at = area(at, D)

        def slot(n):
            return ring[:, (n % RING) * SLOT:(n % RING + 1) * SLOT]

        def chunk(l, kind, j=0):
            return l * PER_LAYER + CHUNK[(kind, j)]

        def loaded(n):
            return st.sem(f'slot{n % RING}_loaded'), 48 * (n // RING + 1)

        def used(n):
            return st.sem('chunks_used'), n + 1

        def kview(v, n):
            return v.rearrange("p (k n) -> p k n", n=n)

        def expert_views(v):
            gu = v[:, 0:2 * KD * FF].rearrange("p (g k n) -> p g k n", g=2, n=FF)
            return gu, v[:, 2 * KD * FF:].rearrange("p (c n) -> p c n", n=D)

        def latent(l):
            return l == DEPTH - 1

        def tiles(l):
            return NLAT if latent(l) else NT

        WIN = [(0, 768, None), (768, 1536, None), (1536, 1632, (2400, 2672)), (1632, 2400, None)]
        PIECES = [(0, 0, 384, [(PA, 0, 0, 256), (PA, 256, 256, 128)]),
                  (0, 384, 768, [(AV, 0, 0, 128), (PB, 0, 128, 256)]),
                  (1, 0, 384, [(PB, 256, 0, 256), (BV, 0, 256, 128)]),
                  (1, 384, 768, [(BV, 128, 0, 128), (CC, 0, 128, 256)]),
                  (2, 0, 368, [(CC, 256, 0, 96), (DZ, 0, 96, 272)])]

        def piece_views(dst, to, src, at_, n, i):
            a, b = dst[:, i, to:to + n], src[:, at_:at_ + n]
            if dst is PA and to == 0:
                return (a.rearrange("p (y x n) -> p x y n", y=2, x=2), b.rearrange("p (x y n) -> p x y n", y=2, x=2))
            return a, b

        block = ctx.enter_context(nc.Block())

        @block.sync
        def _(sp):
            def load_chunk(l, i):
                n, (kind, j) = l * PER_LAYER + i, ring_chunks(0)[i]
                if n >= RING:
                    sp.wait_ge(*freed(n - RING))
                v, s = slot(n), st.sem(f'slot{n % RING}_loaded')

                def put(dst, src):
                    sp.dma_start(dst, src).then_inc(s, 16)

                def by_rows(dst, src):
                    for k0, k1 in ((0, 3), (3, 6), (6, 8)):
                        put(dst[:, k0:k1], src[:, k0:k1])

                if kind == 'ada':
                    by_rows(kview(v, 768), io['w_ada'][l].rearrange("(k p) n -> p k n", p=P)[:, :, 768 * j:768 * j + 768])
                if kind == 'in':
                    src = io['w_in'][l].rearrange("(k p) n -> p k n", p=P)
                    a, b, more = WIN[j]
                    if more:
                        dst = kview(v[:, 0:KD * 368], 368)
                        put(dst[:, :, 0:b - a], src[:, :, a:b])
                        for k in (0, 4):
                            put(dst[:, k:k + 4, b - a:368], src[:, k:k + 4, more[0]:more[1]])
                    else:
                        by_rows(kview(v, 768), src[:, :, a:b])
                if kind == 'mla':
                    for q in range(2):
                        put(v[0:96, 384 * q:384 * q + 384], io['mla_w_uq'][l, 96 * q:96 * q + 96, :])
                    put(v[:, 768:1280], io['mla_w_ukv'][l])
                if kind == 'out':
                    by_rows(kview(v[:, 0:KD * 512], 512), io['w_out'][l].rearrange("(k p) n -> p k n", p=P)[:, :, 512 * j:512 * j + 512])
                if kind == 'router':
                    by_rows(kview(v[:, 0:KD * NE], NE), io['moe_w_router'][l].rearrange("(k p) n -> p k n", p=P))
                if kind == 'shared':
                    gu, dn = expert_views(v)
                    put(gu[:, 0], io['shared_w_gate'][l].rearrange("(k p) n -> p k n", p=P))
                    put(gu[:, 1], io['shared_w_up'][l].rearrange("(k p) n -> p k n", p=P))
                    put(dn, io['shared_w_down'][l].rearrange("(k p) n -> p k n", p=P))

            def freed(n):
                l, (kind, j) = n // PER_LAYER, ring_chunks(0)[n % PER_LAYER]
                if kind == 'expert':
                    return st.sem(f'expert_done{l}'), j + 1
                if kind == 'in' and j == 3:
                    return after('DVE', 'gdn.end', l)
                return after('PE', *{'ada': ('mod.chunk', l, j), 'in': ('proj.unit', l, (1, 3, 4)[j % 3], NT - 1),
                                     'mla': ('up.unit', l, 7), 'out': ('out.unit', l, 4 * j + 3),
                                     'router': ('rt.logits', l, tiles(l) - 1), 'shared': ('sh.down', l, KD - 1)}[kind])

            def load_expert(l, e, s, sem=None):
                gu, dn = expert_views(slot(s))
                sem = sem or st.sem(f'slot{s % RING}_loaded')
                w = [io[k][l, e] if isinstance(e, int) else io[k][l, bass.ds(e, 1)].rearrange("o a b -> (o a) b")
                     for k in ('moe_w_gate', 'moe_w_up', 'moe_w_down')]
                sp.dma_start(gu[:, 0], w[0].rearrange("(p k) n -> p k n", k=KD)).then_inc(sem, 16)
                sp.dma_start(gu[:, 1], w[1].rearrange("(p k) n -> p k n", k=KD)).then_inc(sem, 16)
                sp.dma_start(dn, w[2].rearrange("(p k) n -> p k n", k=2)).then_inc(sem, 16)

            sp.dma_start(cst[:], io['cst']).then_inc(*done('DMA', 'cst.all', 0, by=16))
            for l in range(DEPTH):
                def row(dst, n, src):
                    sp.dma_start(rows[l][dst:dst + n, :], src).then_inc(*done('DMA', 'rows.all', l, dst, by=16))
                r8 = lambda v: v.rearrange("(k p) -> k p", p=P)
                row(0, 48, r8(io['b_ada'][l]))
                row(48, 8, r8(io['norm1_g'][l]))
                row(56, 8, r8(io['norm2_g'][l]))
                row(64, 8, r8(io['final_norm_g']))
                row(72, 8, r8(io['c'][0]))
                row(80, 8, r8(io['c_ctx']))
                row(88, 30, io['gdn_conv_w'][l].rearrange("a (k p) -> (a k) p", p=P))
                if l == 0:
                    for s, name in enumerate(('x', 'ctx')):
                        sp.dma_start(x_rows[:, 2 * s:2 * s + 2, :], io[name][0].rearrange("(i p) n -> p i n", p=P)
                                     ).then_inc(*done('DMA', 'x.rows', 0, s, by=16))
                    for i in range(3):
                        load_chunk(0, i)
            for l in range(DEPTH):
                q = 0
                for name in ('mla_q_norm_g', 'mla_kv_norm_g', 'diff_norm_g', 'gdn_norm_g', 'swa_sinks', 'moe_bias',
                             'diff_lq1', 'diff_lq2', 'diff_lk1', 'diff_lk2',
                             'gdn_a_log_f', 'gdn_a_log_b', 'gdn_dt_bias_f', 'gdn_dt_bias_b'):
                    src = io[name][l:l + 1, :]
                    n = src.shape[1]
                    sp.dma_start(bc[l][:, q:q + n], io[name][l].partition_broadcast(P)
                                 ).then_inc(*done('DMA', 'bc.all', l, name, by=16))
                    q += n
                assert q == BCW

            for l in range(DEPTH):
                for i in range(3 if l == 0 else 0, CHUNK[('expert', 0)]):
                    load_chunk(l, i)
                base = chunk(l, 'expert')
                for e in range(RING):
                    sp.wait_ge(*freed(base + e - RING))
                    load_expert(l, e, base + e)
                with sp.Fori(0, (NE - RING) // RING) as j:
                    for u in range(RING):
                        sp.wait_ge(st.sem(f'expert_done{l}'), RING * j + u + 1)
                        load_expert(l, RING * j + (RING + u), base + u)
                for e in range(NE - (NE - RING) % RING, NE):
                    sp.wait_ge(*freed(base + e - RING))
                    load_expert(l, e, base + e)
                more = tiles(l) * P // CAP - 1
                sp.wait_ge(*after('DVE', 'rt.flag', l))
                with sp.If(sp.value_load(flags[0:1, l:l + 1], min_val=0, max_val=NE * CODES) > 0):
                    with sp.Fori(0, NE) as e:
                        sp.wait_ge(st.sem(f'expert_done{l}'), more * e + NE)
                        load_expert(l, e, base, st.sem(f'more_loaded_{l}'))
                    sp.wait_ge(st.sem(f'expert_done{l}'), NE * (more + 1))
        SCAN = {
            'rb': [('Pool', 'scan.cum')], 'kk': [], 'qk': [],
            'bt': [('DVE', 'scan.b')], 'attt': [('DVE', 'scan.att')],
            'b2': [('ACT', 'scan.bt')], 'b2t': [('ACT', 'scan.bt')],
            'z1': [('DVE', 'scan.b2'), ('DVE', 'scan.z')],
            'b4': [('ACT', 'scan.b2t'), ('DVE', 'scan.b2')], 'b4t': [('ACT', 'scan.b2t')],
            'z2': [('ACT', 'scan.b4'), ('DVE', 'scan.z1')], 'b8': [('ACT', 'scan.b4t')],
            'z3': [('ACT', 'scan.b8'), ('DVE', 'scan.z2')],
            'm': [('DVE', 'scan.z3'), ('Pool', 'scan.n')], 'mt': [('DVE', 'scan.z3')],
            'x0': [('Pool', 'scan.rk')],
            'm2': [('ACT', 'scan.m'), ('ACT', 'scan.mt')], 'm2t': [('ACT', 'scan.mt')],
            'm4t': [('ACT', 'scan.m2'), ('DVE', 'scan.m2t')],
            'x1': [('ACT', 'scan.m4t'), ('ACT', 'scan.x0')], 'x2': [('DVE', 'scan.x1')],
            'u': [('DVE', 'scan.x2'), ('DVE', 'scan.imt')], 'wt': [('DVE', 'scan.x2')],
            'qgt': [('Pool', 'scan.qg')], 'ws': [('ACT', 'scan.wt')],
            'o': [('DVE', 'scan.vnew'), ('ACT', 'scan.attt')],
            'sn': [('DVE', 'scan.vnew'), ('Pool', 'scan.kdec')]}
        TAKEN = {n: [('DVE', 'scan.' + n)] for n in ('b2', 'z1', 'z2', 'z3', 'm2t', 'x1', 'x2', 'u', 'sn')}
        TAKEN |= {n: [('ACT', 'scan.' + n)] for n in ('attt', 'b2t', 'b4', 'b4t', 'b8', 'm', 'x0', 'm2', 'm4t', 'wt', 'qgt')}
        TAKEN |= {'rb': [('DVE', 'scan.dd'), ('ACT', 'scan.egl')], 'kk': [('DVE', 'scan.kk')], 'qk': [('DVE', 'scan.att')],
                  'bt': [('ACT', 'scan.bt'), ('DVE', 'scan.z')], 'mt': [('ACT', 'scan.mt'), ('DVE', 'scan.imt')],
                  'ws': [('DVE', 'scan.vnew')], 'o': [('DVE', 'scan.o'), ('ACT', 'scan.o')]}

        def skip_scan(l, s, d, name):
            unread = scan_tile(s, d) >= tiles(l)
            return ((name == 'ws' and s == 0) or (name == 'qgt' and (s == 0 or unread))
                    or (name in ('qk', 'att', 'attt', 'o') and unread) or (name == 'sn' and s == 3))

        def scan_bank(name, d):
            return 4 * d + list(SCAN).index(name) % 4

        def scan_free(l, s, d, name):
            order = [(a, b) for a in range(4) for b in SCAN if not skip_scan(l, a, d, b)]
            for a, b in reversed(order[:order.index((s, name))]):
                if scan_bank(b, d) == scan_bank(name, d):
                    if b == 'o':
                        return [('ACT' if a % 2 == 0 else 'DVE', 'scan.o', l, a, d)]
                    if b in ('ws',) and a == 0:
                        return []
                    return [(e, n, l, a, d) for e, n in TAKEN[b]]
            return [('DVE', 'gc.out', l)]

        def m_sem(l, name):
            return st.sem(f'{name}_{l}')

        IN_SLOT0 = len(range(0, NE, RING))

        def nth_dma(nth, r):
            return 16 * nth + 16

        DVE_SCAN = ('dd', 'big', 'kk', 'kb', 'b', 'att', 'z', 'b2', 'z1', 'z2', 'z3', 'imt', 'm2t', 'x1', 'x2', 'u', 'vnew', 'o',
                    'sdec', 'sn')
        ACT_SCAN = ('eg', 'egl', 'ekd', 'dec', 'bt', 'attt', 'b2t', 'b4', 'b4t', 'b8', 'm', 'mt', 'x0', 'm2', 'm4t', 'wt', 'qgt', 'o')
        POOL_SCAN = ('cum', 'beg', 'rv', 'rk', 'n', 'qg', 'kdec')

        def first_visit(i, d):
            return next((s, 1 - d) for s in range(4) if scan_tile(s, 1 - d) == i)

        def moe_walk(engine, first, rows, out, inner):
            rows(0, 0)
            first(0, 0)
            rows(1, 1)
            inner(0, 0)
            loops = (NE - 2) // RING

            def three(j):
                for u in range(RING):
                    e = RING * j + (u + 1)
                    first(e, (u + 1) % RING)
                    rows(e + 1, (u + 2) % RING)
                    out(e - 1, u, 16 * j)
                    inner(e, (u + 1) % RING)

            three(0)
            with engine.Fori(1, loops) as j:
                three(j)
            for e in range(RING * loops + 1, NE + 1):
                if e < NE:
                    first(e, e % RING)
                if e + 1 < NE:
                    rows(e + 1, (e + 1) % RING)
                out(e - 1, (e - 1) % RING, 16 * ((e - 1) // RING))
                if e < NE:
                    inner(e, e % RING)
        TR = ([(lambda i, h=h: PA[:, i, P * h:P * h + P], QAT[:, h], P, 64 ** -0.5)
               for h in range(2)]
              + [(lambda i: PA[:, i, 256:384], KAT, P, 1.0)]
              + [(lambda i, q=q: PB[:, i, P * q:P * q + P], DQT[:, q], P, 32 ** -0.5) for q in range(2)]
              + [(lambda i, q=q: PB[:, i, 256 + P * q:256 + P * q + P], DKT[:, q], P, 1.0) for q in range(2)]
              + [(lambda i, q=q: CC[:, i, 96 * q:96 * q + 96], CQT[:, q], 96, 1.0) for q in range(2)]
              + [(lambda i: CC[:, i, 192:320], CKT, P, 1.0)])
        TM = ([(lambda i, h=h: QM[:, i, 96 * h:96 * h + 96], QMT[:, h], 96, 96 ** -0.5) for h in range(4)]
              + [(lambda i, h=h: KF[:, 4 * i + h, :], KMT[:, h], 96, 1.0) for h in range(4)])

        def evac_engine(n):
            return 'ACT' if n % 2 == 0 else 'DVE'

        def attention_map(i, m):
            keys = slice(0, T) if i < NLAT else slice(SEQ, T)
            q = slice(P * i, P * i + P)
            if m < 4:
                b = 64 * (m // 2)
                return (QAT[b:b + 64, m % 2, q], KAT[b:b + 64, keys], lambda kt: AV[:, kt, 64 * (m // 2):64 * (m // 2) + 64])
            if m < 8:
                h = m - 4
                return QMT[:, h, q], KMT[:, h, keys], lambda kt: KV[:, kt, 128 * h + 64:128 * h + 128]
            n = m - 8
            b = 32 * (n % 4)
            return (DQT[b:b + 32, n // 4, q], DKT[b:b + 32, n // 4, keys], lambda kt: BV[:, kt, 64 * (n // 2):64 * (n // 2) + 64])

        def key_tiles(i):
            return list(range(NT)) if i < NLAT else list(range(NLAT, NT))

        def scan_tile(s, d):
            return ((2, 3, 0, 1), (3, 2, 1, 0))[d][s]

        def o_bank(i, m):
            return bank[4 + 2 * (i % 2) + m // 8]


        @block.tensor
        def _(pe):
            def mm(o, a, b, first=True, last=True):
                return pe.matmul(o, a, b, start=first, stop=last)

            def tr(o, a):
                return pe.transpose(o, a, ident[0:a.shape[0], 0:a.shape[0]])

            def wait(*step):
                pe.wait_ge(*after(*step))

            def squares_sum(l, norm, n):
                for c in range(KD):
                    wait('ACT', norm + '.sq', l, c)
                    last = mm(bank[6][:, 0:n], ones, hT[:, c, 0:n], c == 0, c == KD - 1)
                last.then_inc(*done('PE', norm + '.sum', l))

            wait('DMA', 'cst.all', 0)
            for l in range(DEPTH):
                wait('DMA', 'rows.all', l, 88)
                last = tr(bank[0][:, 256 * l:256 * l + 118], rows[l][0:118, :])
            last.then_inc(*done('PE', 'start.cols', 0))
            wait('DMA', 'x.rows', 0, 1)
            for c in range(KD):
                if c == 7:
                    wait('DVE', 'start.cols', 0, 1)
                for i in range(NT):
                    last = tr(bank[(c + 1) % 8][:, P * i:P * i + P], x_rows[:, i, P * c:P * c + P])
                last.then_inc(*done('PE', 'start.x', 0, c))

            for l in range(DEPTH):
                n_tok = P * tiles(l)

                if l == 0:
                    wait('ACT', 'start.sc', 0)
                    wait(evac_engine(6), 'start.x', 0, 6)
                for j in range(8):
                    pe.wait_ge(*loaded(chunk(l, 'ada', j)))
                    w = kview(slot(chunk(l, 'ada', j)), 768)
                    for m in range(6):
                        for k in range(KD):
                            q = 2 * (6 * j + m)
                            last = mm(bank[7][:, q:q + 2], w[:, k, P * m:P * m + P], SC[:, k, :], k == 0, k == KD - 1)
                    last.then_inc(*done('PE', 'mod.chunk', l, j))

                squares_sum(l, 'norm1', T)

                wait('ACT', 'norm1.bias', l, KD - 1)
                for pi, (j, a, b, _) in enumerate(PIECES):
                    n = chunk(l, 'in', j)
                    pe.wait_ge(*loaded(n))
                    width = 368 if j == 2 else 768
                    w = kview(slot(n)[:, 0:KD * width], width)
                    for i in range(NT):
                        u = NT * pi + i
                        if u >= 4:
                            wait(evac_engine(u), 'proj.out', l, u - 4)
                        for k in range(KD):
                            last = mm(bank[u % 4][:, 0:b - a], hT[:, k, P * i:P * i + P], w[:, k, a:b], k == 0, k == KD - 1)
                        last.then_inc(*done('PE', 'proj.unit', l, pi, i))
                pe.wait_ge(*loaded(chunk(l, 'in', 3)))
                w = kview(slot(chunk(l, 'in', 3)), 768)
                for m in range(6):
                    u = NT * len(PIECES) + m
                    wait(evac_engine(u), 'proj.out', l, u - 4)
                    for k in range(KD):
                        last = mm(bank[u % 4][:], w[:, k, P * m:P * m + P], hT[:, k, :], k == 0, k == KD - 1)
                    last.then_inc(*done('PE', 'proj.dqkv', l, m))

                for k, (src, _, r, _) in enumerate(TR):
                    if k == 0:
                        wait('DVE', 'rope.a.sum', l)
                    if k == 3:
                        wait('DVE', 'rope.b.sum', l)
                    if 4 <= k < 8:
                        u = (24, 25, 22, 23)[k - 4]
                        wait(evac_engine(u), 'proj.out', l, u)
                    if k == 7:
                        wait('DVE', 'lat.norm', l, NT - 1, 0)
                    if k == 9:
                        wait('DVE', 'lat.norm', l, NT - 1, 1)
                    if k >= 8:
                        wait(evac_engine(k - 8), 'tr.out', l, k - 8)
                    for i in range(NT):
                        last = tr(bank[(k + 4) % 8][0:r, P * i:P * i + P], src(i))
                    last.then_inc(*done('PE', 'tr.unit', l, k))

                pe.wait_ge(*loaded(chunk(l, 'mla')))
                w = slot(chunk(l, 'mla'))
                for v in range(8):
                    i, o = v % 4, bank[(6 + v) % 8]
                    wait(evac_engine(v + 2), 'tr.out', l, v + 2)
                    if v == 0:
                        wait('ACT', 'tr.out', l, 8)
                        wait('DVE', 'tr.out', l, 7)
                    if v < 4:
                        for q in range(2):
                            last = mm(o[:, 0:384], CQT[:, q, P * i:P * i + P], w[0:96, 384 * q:384 * q + 384], q == 0, q == 1)
                    else:
                        if v == 4:
                            wait('DVE', 'tr.out', l, 9)
                        last = mm(o[:], CKT[:, P * i:P * i + P], w[:, 768:1280])
                    last.then_inc(*done('PE', 'up.unit', l, v))
                for k, (src, _, r, _) in enumerate(TM):
                    if k == 0:
                        wait('DVE', 'rope.q.sum', l)
                        wait('ACT', 'up.out', l, 2)
                        wait('DVE', 'up.out', l, 3)
                    if k == 4:
                        wait('Pool', 'kf.rope', l)
                    wait(evac_engine(k), 'up.out', l, k)
                    for i in range(NT):
                        last = tr(bank[(6 + k) % 8][0:r, P * i:P * i + P], src(i))
                    last.then_inc(*done('PE', 'tm.unit', l, k))

                wait('ACT', 'tm.out', l, 6)
                wait('DVE', 'tm.out', l, 7)
                U = 16 * tiles(l)
                for step in range(U + 2):
                    u = step
                    if u < U:
                        i, m = divmod(u, 16)
                        q, k, _ = attention_map(i, m)
                        if u >= 2:
                            wait('ACT', 'att.exp', l, u - 2)
                        mm(bank[u % 2][:, 0:k.shape[-1]], q, k).then_inc(*done('PE', 'att.score', l, u))
                    u = step - 1
                    if 0 <= u < U:
                        i, m = divmod(u, 16)
                        wait('ACT', 'att.exp', l, u)
                        if u >= 2:
                            wait(evac_engine(u), 'att.pt', l, u - 2)
                        for n in range(len(key_tiles(i))):
                            last = tr(bank[2 + u % 2][:, P * n:P * n + P], PX[:, u % 3, P * n:P * n + P])
                        last.then_inc(*done('PE', 'att.pt', l, u))
                    u = step - 2
                    if 0 <= u < U:
                        i, m = divmod(u, 16)
                        wait(evac_engine(u), 'att.pt', l, u)
                        if i >= 2 and m == 0:
                            wait('DVE', 'att.y', l, i - 2, 1)
                        kts = key_tiles(i)
                        for n, kt in enumerate(kts):
                            last = mm(o_bank(i, m)[:, 64 * (m % 8):64 * (m % 8) + 64], PXT[:, u % 3, P * n:P * n + P],
                                      attention_map(i, m)[2](kt), n == 0, n == len(kts) - 1)
                        last.then_inc(*done('PE', 'att.pv', l, u))

                wait('DVE', 'att.y', l, tiles(l) - 1, 1)
                for i in range(NT):
                    for half in range(2):
                        n = 2 * i + half
                        if i == 0:
                            wait('ACT', 'conv.silu', l, 3 if half == 0 else 5)
                        for c in range(4 if half == 0 else 2):
                            last = tr(bank[n][:, P * c:P * c + P], CV[:, 4 * half + c, P * i:P * i + P])
                        last.then_inc(*done('PE', 'gt.unit', l, n))
                wait('DVE', 'qk.norm', l)
                for i in range(NT):
                    for half in range(2):
                        n = 2 * i + half
                        wait(evac_engine(n), 'gt.out', l, n)
                        for h in range(4):
                            last = tr(bank[n][0:64, P * h:P * h + P], GT[:, i, 256 * half + 64 * h:256 * half + 64 * h + 64])
                        last.then_inc(*done('PE', 'gq.unit', l, n))
                wait('DVE', 'gate.g', l)
                wait('ACT', 'gq.out', l, 6)
                wait('DVE', 'gq.out', l, 7)
                for i in range(NT):
                    for d in range(2):
                        q = 8 * i + 4 * d
                        last = mm(bank[0][:, q:q + 4], C('le' if d == 0 else 'ge'), GG[:, i, 4 * d:4 * d + 4])
                last.then_inc(*done('PE', 'gc.unit', l))

                for s in range(4):
                    for name in SCAN:
                        for d in range(2):
                            i, w = scan_tile(s, d), W[d]
                            if skip_scan(l, s, d, name):
                                continue
                            o = bank[scan_bank(name, d)]
                            for step in scan_free(l, s, d, name):
                                wait(*step)
                            for step in SCAN[name]:
                                wait(step[0], step[1], l, s, d)
                            if name == 'o' and s > 0:
                                wait('ACT', 'scan.qgt', l, s, d)
                            if name in ('ws', 'o') and s > 0:
                                wait('DVE', 'scan.sn', l, s - 1, d)
                            for h in range(4):
                                a, b = slice(P * h, P * h + P), slice(64 * h, 64 * h + 64)
                                q, k = GQ[:, i, a], GK[:, i, a]
                                if name == 'rb':
                                    if h == 0:
                                        last = mm(o[:], ones, w['cum'])
                                elif name in ('bt', 'attt'):
                                    last = tr(o[:, a], w['b' if name == 'bt' else 'att'][:, a])
                                elif name == 'qgt':
                                    last = tr(o[0:64, a], w['qg'][:, b])
                                elif name == 'u':
                                    last = mm(o[:, b], w['imt'][:, a], w['x2'][:, P * h:P * h + 64])
                                elif name == 'wt':
                                    last = mm(o[0:64, a], w['x2'][:, P * h + 64:P * h + P], w['imt'][:, a])
                                elif name == 'ws':
                                    last = mm(o[:, b], w['wt'][0:64, a], w['s'][0:64, b])
                                elif name == 'o':
                                    if s > 0:
                                        mm(o[:, b], w['qgt'][0:64, a], w['s'][0:64, b], True, False)
                                    last = mm(o[:, b], w['attt'][:, a], w['vnew'][:, b], s == 0, True)
                                elif name == 'sn':
                                    last = mm(o[0:64, b], w['kdec'][:, b], w['vnew'][:, b])
                                else:
                                    x, y = {'kk': (k, k), 'qk': (q, k), 'b2': ('bt', 'b'), 'b2t': ('b', 'bt'),
                                            'z1': ('b2', 'z'), 'b4': ('b2t', 'b2'), 'b4t': ('b2', 'b2t'), 'z2': ('b4', 'z'),
                                            'b8': ('b4t', 'b4'), 'z3': ('b8', 'z'), 'm': ('z', 'n'), 'mt': ('n', 'z'),
                                            'm2': ('mt', 'm'), 'm2t': ('m', 'mt'), 'm4t': ('m2', 'm2t'), 'x0': ('z', 'r'),
                                            'x1': ('m4t', 'x0'), 'x2': ('m2t', 'x1')}[name]
                                    x, y = (v if not isinstance(v, str) else w[v][:, a] for v in (x, y))
                                    last = mm(o[:, a], x, y)
                            last.then_inc(*done('PE', 'scan.' + name, l, s, d))

                wait('DVE', 'gdn.end', l)
                wait('DVE', 'dif.gain', l)
                for c in range(KD):
                    if c >= 4:
                        wait(evac_engine(c), 'yt.out', l, c - 4)
                    for i in range(tiles(l)):
                        last = tr(bank[c % 4][:, P * i:P * i + P], Y[:, i, P * c:P * c + P])
                    last.then_inc(*done('PE', 'yt.unit', l, c))
                wait('ACT', 'yt.out', l, 6)
                wait('DVE', 'yt.out', l, 7)
                for m in range(KD):
                    n = chunk(l, 'out', m // 4)
                    pe.wait_ge(*loaded(n))
                    w = kview(slot(n)[:, 0:KD * 512], 512)
                    if m >= 4:
                        wait('DVE', 'out.x', l, m - 4, 0)
                    for k in range(KD):
                        last = mm(bank[4 + m % 4][:, 0:n_tok], w[:, k, P * (m % 4):P * (m % 4) + P], YT[:, k, 0:n_tok], k == 0, k == KD - 1)
                    last.then_inc(*done('PE', 'out.unit', l, m))

                wait('DVE', 'out.x', l, 6, 0)
                squares_sum(l, 'norm2', n_tok)
                wait('ACT', 'norm2.bias', l, KD - 1)
                pe.wait_ge(*loaded(chunk(l, 'router')))
                w = kview(slot(chunk(l, 'router'))[:, 0:KD * NE], NE)
                for i in range(tiles(l)):
                    for k in range(KD):
                        last = mm(bank[0][:, NE * i:NE * i + NE], hT[:, k, P * i:P * i + P], w[:, k, :], k == 0, k == KD - 1)
                    last.then_inc(*done('PE', 'rt.logits', l, i))
                for i in range(tiles(l)):
                    for half in range(2):
                        if i >= 1:
                            wait('DVE' if half == 0 else 'ACT', 'rt.rows', l, i - 1, half)
                        for c in range(4):
                            last = tr(bank[2 + half][:, P * c:P * c + P], hT[:, 4 * half + c, P * i:P * i + P])
                        last.then_inc(*done('PE', 'rt.rows', l, i, half))
                n = chunk(l, 'shared')
                pe.wait_ge(*loaded(n))
                gu, dn = expert_views(slot(n))
                wait('DVE', 'out.x', l, KD - 1, 0)
                for f in range(2):
                    for g in range(2):
                        for k in range(KD):
                            last = mm(bank[4 + 2 * f + g][:, 0:n_tok], gu[:, g, k, P * f:P * f + P], hT[:, k, 0:n_tok], k == 0, k == KD - 1)
                        last.then_inc(*done('PE', 'sh.up', l, f, g))
                wait('DVE', 'rt.vc', l)
                for i in range(tiles(l)):
                    last = tr(bank[1][0:NE, P * i:P * i + P], VC[:, i, :])
                last.then_inc(*done('PE', 'rt.vt', l))
                wait('DVE', 'sh.act', l, 1)
                wait('ACT', 'rt.rows', l, tiles(l) - 1, 1)
                wait('DVE', 'rt.rows', l, tiles(l) - 1, 0)
                for m in range(KD):
                    if m >= 2:
                        wait('DVE', 'sh.x', l, m - 2, 0)
                    for c in range(2):
                        last = mm(bank[2 + m % 2][:, 0:n_tok], dn[:, c, P * m:P * m + P], SH2[:, c, 0:n_tok], c == 0, c == 1)
                    last.then_inc(*done('PE', 'sh.down', l, m))
                wait('DVE', 'rt.list', l, CAP // 8 - 1)
                wait('DVE', 'rt.left', l)
                tr(bank[1][:, 0:NE], LST[:, 0:CAP])
                mm(bank[1][:, NE:NE + 1], ones[0:NE, :], LEFT[0:NE]).then_inc(*done('PE', 'rt.slots', l))
                wait('DVE', 'rt.code', l)
                wait('DVE', 'sh.x', l, KD - 1, 0)

                def gather_turn(e, r, nth):
                    pe.wait_ge(m_sem(l, f'xg_loaded{r}'), nth_dma(nth, r))
                    pe.wait_ge(m_sem(l, 'xgT_dve'), e)
                    pe.wait_ge(m_sem(l, 'xgT_act'), e)
                    for c in range(KD):
                        last = tr(bank[c // 4][:, P * (c % 4):P * (c % 4) + P], xg[:, r, c::KD])
                    last.then_inc(m_sem(l, 'xg_turned'), 1)

                def up(e, r, n_loaded, sl):
                    pe.wait_ge(m_sem(l, 'xgT_dve'), e + 1)
                    pe.wait_ge(m_sem(l, 'xgT_act'), e + 1)
                    pe.wait_ge(*n_loaded)
                    gu, _ = expert_views(slot(sl))
                    for k in range(KD):
                        last = mm(bank[2][:].rearrange("p (g n) -> p g n", g=2), xgT[:, r, P * k:P * k + P], gu[:, :, k, :], k == 0, k == KD - 1)
                    last.then_inc(m_sem(l, 'up_done'), 1)

                def inner_turn(e, r):
                    pe.wait_ge(m_sem(l, 'inner_done'), e + 1)
                    for c in range(2):
                        last = tr(bank[3][:, P * c:P * c + P], hh[:, r, c::2])
                    last.then_inc(m_sem(l, 'inner_turned'), 1)

                def down(e, r, sl):
                    pe.wait_ge(m_sem(l, 'hhT_done'), e + 1)
                    if not (isinstance(e, int) and e == 0):
                        pe.wait_ge(m_sem(l, 'yy_dve'), e)
                        pe.wait_ge(m_sem(l, 'yy_act'), e)
                    _, dn = expert_views(slot(sl))
                    for half in range(2):
                        for c in range(2):
                            last = mm(bank[4 + half][:], hhT[:, r, P * c:P * c + P], dn[:, c, 512 * half:512 * half + 512], c == 0, c == 1)
                    last.then_inc(st.sem(f'expert_done{l}'), 1)

                base = chunk(l, 'expert')

                def arrived(e0, j=None):
                    s, v = loaded(base + e0)
                    return (s, v) if j is None else (s, 48 * j + v)

                for c in range(KD):
                    if c == 0:
                        pe.wait_ge(m_sem(l, 'xg_loaded0'), 16)
                    last = tr(bank[c // 4][:, P * (c % 4):P * (c % 4) + P], xg[:, 0, c::KD])
                last.then_inc(m_sem(l, 'xg_turned'), 1)
                up(0, 0, arrived(0), base)
                gather_turn(1, 1, 0)
                inner_turn(0, 0)
                LOOPS = (NE - 2) // RING
                with pe.Fori(0, LOOPS) as j:
                    for u in range(RING):
                        e, r = RING * j + (u + 1), (u + 1) % RING
                        up(e, r, arrived(u + 1, j), base + u + 1)
                        gather_turn(e + 1, (u + 2) % RING, j + (u + 2) // RING)
                        down(e - 1, u, base + u)
                        inner_turn(e, r)
                for e in range(RING * LOOPS + 1, NE + 1):
                    r = e % RING
                    if e < NE:
                        up(e, r, arrived(e), base + e)
                    if e + 1 < NE:
                        gather_turn(e + 1, (e + 1) % RING, (e + 1) // RING)
                    down(e - 1, (e - 1) % RING, base + e - 1)
                    if e < NE:
                        inner_turn(e, r)

                more = n_tok // CAP - 1
                wait('DVE', 'rt.flag', l)
                with pe.If(pe.value_load(flags[0:1, l:l + 1], min_val=0, max_val=NE * CODES) > 0):
                    pe.wait_ge(m_sem(l, 'more_dropped'), more * CAP // 8)
                    for k in range(more):
                        last = tr(bank[6][:, NE * k:NE * k + NE], LST[:, CAP * (k + 1):CAP * (k + 2)])
                    last.then_inc(m_sem(l, 'more_turned'), 1)
                    with pe.Fori(0, NE) as e:
                        for k in range(more):
                            q = more * e + (NE + k)
                            gather_turn(q, 0, more * e + (IN_SLOT0 + k))
                            up(q, 0, (m_sem(l, 'more_loaded'), 48 * e + 48), base)
                            inner_turn(q, 0)
                            down(q, 0, base)

                for i in range(tiles(l)):
                    wait('DVE', 'comb.sum', l, i, TOPK - 1)
                    if i >= 1:
                        wait('DVE', 'comb.x', l, i - 1, KD - 1)
                    for c in range(KD):
                        last = tr(bank[6 + c // 4][:, P * (c % 4):P * (c % 4) + P], YC[:, P * c:P * c + P])
                    last.then_inc(*done('PE', 'comb.turn', l, i))
                wait('DVE', 'comb.x', l, tiles(l) - 1, KD - 1)

            squares_sum(0, 'fin', SEQ)
            wait('DVE', 'fin.scale', 0, KD - 1)
            for i in range(NLAT):
                for half in range(2):
                    for c in range(4):
                        last = tr(bank[2 * i + half][:, P * c:P * c + P], hT[:, 4 * half + c, P * i:P * i + P])
                    last.then_inc(*done('PE', 'fin.turn', 0, i, half))

        @block.vector
        def _(dve):
            def wait(*step):
                dve.wait_ge(*after(*step))

            def copy_out(k, dst, src, factor=1.0):
                if factor == 1.0:
                    return dve.tensor_copy(dst, src)
                return dve.tensor_scalar(dst, src, factor, None, ALU.mult)

            def tt(o, a, b, op=ALU.mult):
                return dve.tensor_tensor(o, a, b, op)

            def stt(o, a, s, b, op0=ALU.mult, op1=ALU.mult):
                return dve.scalar_tensor_tensor(out=o, in0=a, scalar=s, in1=b, op0=op0, op1=op1)

            def bcast(v, *shape):
                return v.unsqueeze(len(v.shape)).broadcast_to(tuple(shape))

            def rope(l, name, v, heads, dim, cos, sin, a, b):
                half = dim // 2
                shape = (P, 2, heads, dim)
                c = cos.rearrange("p (i n) -> p i n", n=dim).unsqueeze(2).broadcast_to(shape)
                s = sin.rearrange("p (i n) -> p i n", n=dim).unsqueeze(2).broadcast_to(shape)
                a = a.rearrange("p (i h n) -> p i h n", i=2, n=dim)
                b = b.rearrange("p (i h n) -> p i h n", i=2, n=dim)
                tt(a, v, c)
                tt(b[:, :, :, 0:half], v[:, :, :, half:dim], s[:, :, :, 0:half])
                tt(b[:, :, :, half:dim], v[:, :, :, 0:half], s[:, :, :, half:dim]).then_inc(*done('DVE', name + '.prod', l))
                wait('DVE', name + '.prod', l)
                tt(v, a, b, ALU.add).then_inc(*done('DVE', name + '.sum', l))

            def inverse_root(l, norm, n):
                wait('ACT', norm + '.root', l)
                dve.reciprocal(v_rt[:, 0:n], v_rs[:, 0:n]).then_inc(*done('DVE', norm + '.rstd', l))
                wait('DVE', norm + '.rstd', l)

            wait('PE', 'start.cols', 0)
            for l in range(DEPTH):
                dve.tensor_copy(cols[l][:], bank[0][:, 256 * l:256 * l + 118]).then_inc(*done('DVE', 'start.cols', 0, l))
            for c in range(1, KD, 2):
                wait('PE', 'start.x', 0, c)
                dve.tensor_copy(xT[:, c], bank[(c + 1) % 8][:]).then_inc(*done('DVE', 'start.x', 0, c))

            for l in range(DEPTH):
                n_tok = P * tiles(l)
                streams = range(2) if not latent(l) else range(1)
                md = mod[l][:].rearrange("p (m g) -> p m g", g=2)
                am = amp[l][:].rearrange("p (n c g) -> p n c g", n=2, g=2)
                b = bc[l]

                wait('PE', 'mod.chunk', l, 7)
                tt(md, bank[7][:, 0:96].rearrange("p (m g) -> p m g", g=2), bcast(cols[l][:, 0:48], P, 48, 2), ALU.add
                   ).then_inc(*done('DVE', 'mod.bias', l))
                wait('DVE', 'mod.bias', l)
                for n in range(2):
                    stt(am[:, n], md[:, 8 + 24 * n:16 + 24 * n], 1.0, bcast(cols[l][:, 48 + 8 * n:56 + 8 * n], P, KD, 2), ALU.add, ALU.mult
                        ).then_inc(*done('DVE', 'mod.gain', l, n))
                lam_init = 0.8 - 0.6 * math.exp(-0.3 * l)
                wait('DMA', 'bc.all', l, 'gdn_dt_bias_b')
                tt(b[:, 516:580], b[:, 516:580], b[:, 580:644]).then_inc(*done('DVE', 'lam.prod', l))
                wait('DVE', 'lam.prod', l)
                dve.tensor_reduce(lamt[:, 0:2], b[:, 516:580].rearrange("p (a n) -> p a n", n=32), AX.X, ALU.add
                                  ).then_inc(*done('DVE', 'lam.sum', l))
                wait('ACT', 'lam.exp', l)
                stt(lamt[:, 4:5], lamt[:, 3:4], -lam_init, lamt[:, 2:3], ALU.add, ALU.subtract).then_inc(*done('DVE', 'lam.neg', l))
                dve.tensor_scalar(b[:, 320:384], b[:, 320:384], 1.0 - lam_init, None, ALU.mult).then_inc(*done('DVE', 'lam.gain', l))

                v_rs, v_rt = rstd_s, rstd_t
                inverse_root(l, 'norm1', T)
                wait('DVE', 'mod.gain', l, 1)
                for c in range(KD):
                    for g in range(2):
                        q = slice(SEQ * g, SEQ * g + SEQ)
                        stt(hT[:, c, q], xT[:, c, q], am[:, 0, c, g:g + 1], rstd_t[:, q]).then_inc(*done('DVE', 'norm1.scale', l, c, g))

                wait('ACT', 'norm1.bias', l, KD - 1)
                wait('Pool', 'pad.zero', l)
                for u in range(NT * len(PIECES) + 6):
                    if evac_engine(u) != 'DVE':
                        continue
                    if u < NT * len(PIECES):
                        pi, i = divmod(u, NT)
                        wait('PE', 'proj.unit', l, pi, i)
                        for dst, to, at_, n in PIECES[pi][3]:
                            last = dve.tensor_copy(*piece_views(dst, to, bank[u % 4], at_, n, i))
                    else:
                        m = u - NT * len(PIECES)
                        wait('PE', 'proj.dqkv', l, m)
                        last = dve.tensor_copy(GP[:, m].rearrange("p (g n) -> p g n", g=2)[:, :, 2:258],
                                               bank[u % 4][:].rearrange("p (g n) -> p g n", g=2))
                    last.then_inc(*done('DVE', 'proj.out', l, u))
                    if u == 15:
                        wait('ACT', 'proj.out', l, 12)
                        wait('DVE', 'proj.out', l, 13)
                        rope(l, 'rope.a', PA[:, 0:2, :].rearrange("p i (h n) -> p i h n", n=64), 6, 64, C('cos_a'), C('sin_a'),
                             tA[:, 0:768], tB[:, 0:768])
                    if u == 17:
                        wait('DVE', 'rope.a.sum', l)
                        rope(l, 'rope.b', PB[:, 0:2, :].rearrange("p i (h n) -> p i h n", n=32), 16, 32, C('cos_b'), C('sin_b'),
                             tA, tB)
                wait('ACT', 'lat.root', l)
                dve.reciprocal(SST[:, :, 2:4], SST[:, :, 2:4]).then_inc(*done('DVE', 'lat.rstd', l))
                wait('DVE', 'rope.b.sum', l)
                rope(l, 'rope.k', CC[:, 0:2, 320:352].rearrange("p i (h n) -> p i h n", n=32), 1, 32, C('cos_b'), C('sin_b'),
                     tA[:, 0:64], tB[:, 0:64])
                wait('DVE', 'lat.rstd', l)
                for i in range(NT):
                    for q, (a_, n_) in enumerate(((0, 192), (192, 128))):
                        stt(CC[:, i, a_:a_ + n_], CC[:, i, a_:a_ + n_], SST[:, i, 2 + q:3 + q], b[:, a_:a_ + n_]
                            ).then_inc(*done('DVE', 'lat.norm', l, i, q))
                wait('PE', 'tr.unit', l, 0)
                for k in range(1, len(TR), 2):
                    _, dst, r, f = TR[k]
                    wait('PE', 'tr.unit', l, k)
                    copy_out(k, dst[0:r], bank[(k + 4) % 8][0:r, :], f).then_inc(*done('DVE', 'tr.out', l, k))
                for v in range(1, 8, 2):
                    wait('PE', 'up.unit', l, v)
                    o = bank[(6 + v) % 8]
                    (dve.tensor_copy(QM[:, v, :], o[:, 0:384]) if v < 4 else dve.tensor_copy(KV[:, v - 4, :], o[:])
                     ).then_inc(*done('DVE', 'up.out', l, v))
                    if v == 1:
                        wait('ACT', 'up.out', l, 0)
                        wait('DVE', 'up.out', l, 1)
                        rope(l, 'rope.q', QM[:, 0:2, :].rearrange("p i (h n) -> p i h n", n=96)[:, :, :, 64:96], 4, 32, C('cos_b'),
                             C('sin_b'), SM[:, 0:256], SM[:, 256:512])
                for k in range(1, len(TM), 2):
                    _, dst, r, f = TM[k]
                    wait('PE', 'tm.unit', l, k)
                    if k == 1:
                        wait('Pool', 'kf.rope', l)
                    copy_out(k, dst[0:r], bank[(6 + k) % 8][0:r, :], f).then_inc(*done('DVE', 'tm.out', l, k))

                U = 16 * tiles(l)
                for step in range(U + 2 + 2):
                    u = step
                    if u < U:
                        i, m = divmod(u, 16)
                        n_keys = P * len(key_tiles(i))
                        wait('PE', 'att.score', l, u)
                        src = bank[u % 2][:, 0:n_keys]
                        if m >= 4:
                            dve.tensor_reduce(NEGM[:, i, m:m + 1], src, AX.X, ALU.max, negate=True).then_inc(*done('DVE', 'att.max', l, u))
                        else:
                            if i < NLAT:
                                if m >= 1:
                                    wait('ACT', 'att.exp', l, u - 1)
                                dve.tensor_tensor_reduce(out=SM, in0=src, in1=C('swa')[:, T * i:T * i + T], scale=1.0, scalar=-3e38,
                                                         op0=ALU.add, op1=ALU.max, accum_out=RINV[:, i, m:m + 1]
                                                         ).then_inc(*done('DVE', 'att.rowmax', l, u))
                            else:
                                dve.tensor_reduce(RINV[:, i, m:m + 1], src, AX.X, ALU.max).then_inc(*done('DVE', 'att.rowmax', l, u))
                            wait('DVE', 'att.rowmax', l, u)
                            dve.tensor_scalar(NEGM[:, i, m:m + 1], RINV[:, i, m:m + 1], b[:, 448 + m:449 + m], -1.0, ALU.max, ALU.mult
                                              ).then_inc(*done('DVE', 'att.max', l, u))
                    u = step - 1
                    if 0 <= u < U and evac_engine(u) == 'DVE':
                        i, m = divmod(u, 16)
                        n = P * len(key_tiles(i))
                        wait('PE', 'att.pt', l, u)
                        if u >= 3:
                            wait('PE', 'att.pv', l, u - 3)
                        dve.tensor_copy(PXT[:, u % 3, 0:n], bank[2 + u % 2][:, 0:n]).then_inc(*done('DVE', 'att.pt', l, u))
                    if step >= 19 and (step - 19) % 16 == 0:
                        i = (step - 19) // 16
                        wait('DVE', 'att.max', l, 16 * i + 3)
                        tt(ESINK[:, i, :], NEGM[:, i, 0:4], b[:, 448:452], ALU.add).then_inc(*done('DVE', 'att.sink', l, i))
                        wait('ACT', 'att.sink', l, i)
                        tt(SUMS[:, i, 0:4], SUMS[:, i, 0:4], ESINK[:, i, :], ALU.add).then_inc(*done('DVE', 'att.sum', l, i))
                        wait('DVE', 'att.sum', l, i)
                        wait('ACT', 'att.exp', l, 16 * i + 15)
                        dve.reciprocal(RINV[:, i, :], SUMS[:, i, :]).then_inc(*done('DVE', 'att.rinv', l, i))
                        wait('DVE', 'att.rinv', l, i)
                        wait('PE', 'att.pv', l, 16 * i + 15)
                        y4 = Y[:, i, :].rearrange("p (a n) -> p a n", a=2)[:, :, 0:256].rearrange("p a (h n) -> p a h n", n=64)
                        tt(y4, o_bank(i, 0)[:].rearrange("p (a h n) -> p a h n", a=2, n=64),
                           RINV[:, i, 0:8].rearrange("p (a h) -> p a h", a=2).unsqueeze(3).broadcast_to((P, 2, 4, 64))
                           ).then_inc(*done('DVE', 'att.y', l, i, 0))
                        if i > 0:
                            wait('DVE', 'att.dif', l, i - 1)
                        dt = CQT0.rearrange("p (h n) -> p h n", n=64)
                        tt(dt, o_bank(i, 8)[:].rearrange("p (h n) -> p h n", n=64), bcast(RINV[:, i, 8:16], P, 8, 64)
                           ).then_inc(*done('DVE', 'att.y', l, i, 1))
                        wait('DVE', 'att.y', l, i, 1)
                        wait('DVE', 'lam.neg', l)
                        stt(Y[:, i, 256:512].rearrange("p (h n) -> p h n", n=64), dt[:, 1::2, :], lamt[:, 4:5], dt[:, 0::2, :], ALU.mult, ALU.add
                            ).then_inc(*done('DVE', 'att.dif', l, i))
                nt = tiles(l)
                yd = Y[:, 0:nt, 256:512].rearrange("p i (h n) -> p i h n", n=64)
                wait('ACT', 'dif.sq', l)
                dve.tensor_reduce(GNS[:, 0:4 * nt], DSQ[:, 0:4 * nt, :], AX.X, ALU.add).then_inc(*done('DVE', 'dif.ss', l))
                wait('ACT', 'dif.root', l)
                dve.reciprocal(GNS[:, 0:4 * nt], GNS[:, 0:4 * nt]).then_inc(*done('DVE', 'dif.rstd', l))
                wait('DVE', 'dif.rstd', l)
                tt(yd, yd, GNS[:, 0:4 * nt].rearrange("p (i h) -> p i h", h=4).unsqueeze(3).broadcast_to((P, nt, 4, 64))
                   ).then_inc(*done('DVE', 'dif.norm', l))
                wait('DVE', 'dif.norm', l)
                tt(yd, yd, b[:, 320:384].unsqueeze(1).unsqueeze(1).broadcast_to((P, nt, 4, 64))).then_inc(*done('DVE', 'dif.gain', l))

                wait('ACT', 'proj.out', l, 24)
                wait('DVE', 'proj.out', l, 25)
                wait('PE', 'att.pv', l, U - 1)
                for tap in range(5):
                    for c in range(6):
                        src = GP[:, c].rearrange("p (g n) -> p g n", g=2)[:, :, tap:tap + 256]
                        dst = CV[:, c].rearrange("p (g n) -> p g n", g=2)
                        wgt = cols[l][:, 88 + 6 * tap + c:89 + 6 * tap + c]
                        if tap == 0:
                            last = dve.tensor_scalar(dst, src, wgt, None, ALU.mult)
                        else:
                            wait('DVE', 'conv.tap', l, tap - 1, c)
                            last = stt(dst, src, wgt, dst, ALU.mult, ALU.add)
                        last.then_inc(*done('DVE', 'conv.tap', l, tap, c))
                ga, gb = DZ[:, :, 256:264], DZ[:, :, 264:272]
                per_tile = lambda v: v.unsqueeze(1).broadcast_to((P, NT, 8))
                tt(GA, ga, per_tile(b[:, 652:660]), ALU.add).then_inc(*done('DVE', 'gate.a', l))
                wait('DVE', 'gate.a', l)
                dve.tensor_scalar(GN, GA, -1.0, None, ALU.mult).then_inc(*done('DVE', 'gate.n', l))
                wait('DVE', 'gate.n', l)
                tt(GN, GN, GA, ALU.min).then_inc(*done('DVE', 'gate.min', l))
                wait('ACT', 'gate.beta', l)
                dve.tensor_scalar(GB, GB, 1.0, None, ALU.add).then_inc(*done('DVE', 'gate.b1', l))
                wait('DVE', 'gate.b1', l)
                dve.reciprocal(GB, GB).then_inc(*done('DVE', 'gate.beta', l))
                wait('ACT', 'gate.ln', l)
                stt(GA, GA, 0.0, GG, ALU.max, ALU.add).then_inc(*done('DVE', 'gate.soft', l))
                wait('DVE', 'gate.soft', l)
                stt(GG, GA, -1.0, per_tile(NEXP)).then_inc(*done('DVE', 'gate.g', l))
                wait('DVE', 'gate.beta', l)
                dve.tensor_scalar(GN, GB, -1.0, None, ALU.mult).then_inc(*done('DVE', 'gate.nb', l))
                for n in range(1, 8, 2):
                    wait('PE', 'gt.unit', l, n)
                    dve.tensor_copy(GT[:, n // 2, 512:768], bank[n][:, 0:256]).then_inc(*done('DVE', 'gt.out', l, n))
                wait('ACT', 'qk.sq', l)
                dve.tensor_reduce(GW, QSQ, AX.X, ALU.add).then_inc(*done('DVE', 'qk.ss', l))
                wait('ACT', 'qk.root', l)
                dve.reciprocal(GW, GW).then_inc(*done('DVE', 'qk.rstd', l))
                wait('DVE', 'qk.rstd', l)
                gw3 = GW.rearrange("p (i h) -> p i h", h=8)
                dve.tensor_scalar(gw3[:, :, 0:4], gw3[:, :, 0:4], 64 ** -0.5, None, ALU.mult).then_inc(*done('DVE', 'qk.qscale', l))
                wait('DVE', 'qk.qscale', l)
                qk = GT[:, :, 0:512].rearrange("p i (h n) -> p i h n", n=64)
                tt(qk, qk, gw3.unsqueeze(3).broadcast_to((P, NT, 8, 64))).then_inc(*done('DVE', 'qk.norm', l))
                for n in range(1, 8, 2):
                    wait('PE', 'gq.unit', l, n)
                    dve.tensor_copy(GK[:, n // 2, :], bank[n][0:64, :]).then_inc(*done('DVE', 'gq.out', l, n))
                wait('PE', 'gc.unit', l)
                dve.tensor_copy(GC, bank[0][:, 0:32].rearrange("p (i n) -> p i n", n=8)).then_inc(*done('DVE', 'gc.out', l))

                heads = lambda v: v.rearrange("p (h n) -> p h n", h=4)
                for s in range(4):
                    for name in DVE_SCAN:
                        for d in range(2):
                            i, w = scan_tile(s, d), W[d]
                            o = lambda x: bank[scan_bank(x, d)]
                            step = ('DVE', 'scan.' + name, l, s, d)
                            over = (P, 4, P)
                            if name in ('att', 'o') and skip_scan(l, s, d, name):
                                continue
                            if name == 'o' and s % 2 == 0 or name == 'sn' and s == 3:
                                continue
                            if name == 'dd':
                                wait('PE', 'scan.rb', l, s, d)
                                wait('DVE', 'gc.out', l)
                                if s > 0 and not skip_scan(l, s - 1, d, 'attt'):
                                    wait('PE', 'scan.attt', l, s - 1, d)
                                last = tt(heads(w['att']), heads(o('rb')[:]), bcast(GC[:, i, 4 * d:4 * d + 4], *over), ALU.subtract)
                            elif name == 'big':
                                wait('DVE', 'scan.dd', l, s, d)
                                last = tt(heads(w['dec']), heads(w['att']), C('big_f' if d == 0 else 'big_b').unsqueeze(1).broadcast_to(over), ALU.add)
                            elif name == 'kk':
                                wait('ACT', 'scan.dec', l, s, d)
                                wait('PE', 'scan.kk', l, s, d)
                                last = tt(w['kd'], o('kk')[:], w['dec'])
                            elif name == 'kb':
                                wait('DVE', 'scan.kk', l, s, d)
                                wait('DVE', 'gate.nb', l)
                                last = tt(heads(w['kd']), heads(w['kd']), bcast(GN[:, i, 4 * d:4 * d + 4], *over))
                            elif name == 'b':
                                wait('DVE', 'scan.kb', l, s, d)
                                last = tt(heads(w['b']), heads(w['kd']), C('in_f' if d == 0 else 'in_b').unsqueeze(1).broadcast_to(over))
                            elif name == 'att':
                                wait('PE', 'scan.qk', l, s, d)
                                wait('ACT', 'scan.ekd', l, s, d)
                                last = tt(w['att'], o('qk')[:], w['dec'])
                            elif name in ('z', 'imt'):
                                src = 'bt' if name == 'z' else 'mt'
                                wait('ACT', 'scan.' + src, l, s, d)
                                last = tt(heads(w[name]), heads(o(src)[:]), ident.unsqueeze(1).broadcast_to(over), ALU.add)
                            elif name in ('z1', 'z2', 'z3'):
                                wait('PE', 'scan.' + name, l, s, d)
                                last = tt(w['z'], o(name)[:], w['z'], ALU.add)
                            elif name in ('x1', 'x2'):
                                wait('PE', 'scan.' + name, l, s, d)
                                last = tt(w[name], o(name)[:], w['x0' if name == 'x1' else 'x1'], ALU.add)
                            elif name in ('b2', 'm2t'):
                                wait('PE', 'scan.' + name, l, s, d)
                                last = dve.tensor_copy(w[name], o(name)[:])
                            elif name == 'u':
                                wait('PE', 'scan.u', l, s, d)
                                last = dve.tensor_copy(w['u'], o('u')[:, 0:256])
                            elif name == 'vnew':
                                wait('DVE', 'scan.u', l, s, d)
                                if s == 0:
                                    last = dve.tensor_copy(w['vnew'], w['u'])
                                else:
                                    wait('PE', 'scan.ws', l, s, d)
                                    last = tt(w['vnew'], w['u'], o('ws')[:, 0:256], ALU.subtract)
                            elif name == 'o':
                                wait('PE', 'scan.o', l, s, d)
                                yg = Y[:, i, 768:1024]
                                wait('ACT', 'scan.o', l, *first_visit(i, d))
                                last = tt(yg, o('o')[:, 0:256], yg, ALU.add)
                            elif name == 'sdec':
                                if s == 0 or s == 3:
                                    continue
                                wait('ACT', 'scan.egl', l, s, d)
                                wait('PE', 'scan.sn', l, s, d)
                                last = tt(w['stmp'][0:64].rearrange("p (h n) -> p h n", h=4), w['s'][0:64].rearrange("p (h n) -> p h n", h=4),
                                          bcast(w['egl'][0:64], 64, 4, 64))
                            elif name == 'sn':
                                wait('PE', 'scan.sn', l, s, d)
                                if s == 0:
                                    last = dve.tensor_copy(w['s'][0:64], o('sn')[0:64, 0:256])
                                else:
                                    wait('DVE', 'scan.sdec', l, s, d)
                                    last = tt(w['s'][0:64], o('sn')[0:64, 0:256], w['stmp'][0:64], ALU.add)
                            last.then_inc(*done(*step))
                yg = Y[:, 0:nt, 768:1024].rearrange("p i (h n) -> p i h n", n=64)
                wait('ACT', 'gout.sq', l)
                dve.tensor_reduce(GNS[:, 0:4 * nt], GSQ[:, 0:4 * nt, :], AX.X, ALU.add).then_inc(*done('DVE', 'gout.ss', l))
                wait('ACT', 'gout.root', l)
                dve.reciprocal(GNS[:, 0:4 * nt], GNS[:, 0:4 * nt]).then_inc(*done('DVE', 'gout.rstd', l))
                wait('DVE', 'gout.rstd', l)
                tt(yg, yg, GNS[:, 0:4 * nt].rearrange("p (i h) -> p i h", h=4).unsqueeze(3).broadcast_to((P, nt, 4, 64))
                   ).then_inc(*done('DVE', 'gout.norm', l))
                wait('DVE', 'gout.norm', l)
                tt(yg, yg, b[:, 384:448].unsqueeze(1).unsqueeze(1).broadcast_to((P, nt, 4, 64))).then_inc(*done('DVE', 'gout.gain', l))
                wait('DVE', 'gout.gain', l)
                wait('ACT', 'gout.z', l)
                tt(Y[:, 0:nt, 768:1024], Y[:, 0:nt, 768:1024], DZ[:, 0:nt, 0:256]).then_inc(*done('DVE', 'gdn.end', l))

                for c in range(1, KD, 2):
                    wait('PE', 'yt.unit', l, c)
                    dve.tensor_copy(YT[:, c, 0:n_tok], bank[c % 4][:, 0:n_tok]).then_inc(*done('DVE', 'yt.out', l, c))
                for m in range(KD):
                    wait('PE', 'out.unit', l, m)
                    for g in reversed(streams):
                        q = slice(SEQ * g, SEQ * g + SEQ)
                        stt(xT[:, m, q], bank[4 + m % 4][:, q], md[:, 16 + m, g:g + 1], xT[:, m, q], ALU.mult, ALU.add
                            ).then_inc(*done('DVE', 'out.x', l, m, g))
                v_rs, v_rt = rstd2_s, rstd2_t
                inverse_root(l, 'norm2', n_tok)
                for c in range(KD):
                    for g in streams:
                        q = slice(SEQ * g, SEQ * g + SEQ)
                        stt(hT[:, c, q], xT[:, c, q], am[:, 1, c, g:g + 1], rstd2_t[:, q]).then_inc(*done('DVE', 'norm2.scale', l, c, g))

                for i in range(nt):
                    wait('PE', 'rt.rows', l, i, 0)
                    if i >= 2:
                        wait('DMA', f'h2row{i % 2}.out', l, i - 2)
                    dve.tensor_copy(HR[:, i % 2, 0:512], bank[2][:]).then_inc(*done('DVE', 'rt.rows', l, i, 0))
                lg, ch = LG[:, 0:nt], CH[:, 0:nt]
                wait('ACT', 'rt.sig', l)
                tt(ch, lg, b[:, 452:516].unsqueeze(1).broadcast_to((P, nt, NE)), ALU.add).then_inc(*done('DVE', 'rt.choice', l))
                wait('DVE', 'rt.choice', l)
                for i in range(nt):
                    for g in range(NG):
                        last = dve.max(TOP8[:, 8 * i + g, :], CH[:, i, 8 * g:8 * g + 8])
                last.then_inc(*done('DVE', 'rt.top2', l))
                wait('DVE', 'rt.top2', l)
                tt(GSC[:, 0:nt], TOP8[:, 0:8 * nt, 0].rearrange("p (i g) -> p i g", g=8), TOP8[:, 0:8 * nt, 1].rearrange("p (i g) -> p i g", g=8),
                   ALU.add).then_inc(*done('DVE', 'rt.group', l))
                wait('DVE', 'rt.group', l)
                for i in range(nt):
                    last = dve.max(GT8[:, i, :], GSC[:, i, :])
                last.then_inc(*done('DVE', 'rt.gtop', l))
                wait('DVE', 'rt.gtop', l)
                for i in range(nt):
                    last = dve.max_index(GIX[:, i, :].bitcast(mybir.dt.uint32), GT8[:, i, :], GSC[:, i, :])
                last.then_inc(*done('DVE', 'rt.gidx', l))
                wait('DVE', 'rt.gidx', l)
                dve.tensor_copy(GIF[:, 0:nt], GIX[:, 0:nt]).then_inc(*done('DVE', 'rt.gfloat', l))
                wait('DVE', 'rt.gfloat', l)
                for i in range(nt):
                    last = tt(OHG[:, 4 * i:4 * i + 4, :], bcast(GIF[:, i, 0:TOPG], P, TOPG, NG),
                              C('experts')[:, 0:NG].unsqueeze(1).broadcast_to((P, TOPG, NG)), ALU.is_equal)
                last.then_inc(*done('DVE', 'rt.ghot', l))
                wait('DVE', 'rt.ghot', l)
                for i in range(nt):
                    last = dve.tensor_reduce(GMK[:, i, :], OHG[:, 4 * i:4 * i + 4, :].rearrange("p k g -> p g k"), AX.X, ALU.add)
                last.then_inc(*done('DVE', 'rt.gmask', l))
                wait('DVE', 'rt.gmask', l)
                dve.tensor_scalar(GMK[:, 0:nt], GMK[:, 0:nt], -1.0, 1e30, ALU.add, ALU.mult).then_inc(*done('DVE', 'rt.gbig', l))
                wait('DVE', 'rt.gbig', l)
                ch8 = ch.rearrange("p i (g e) -> p i g e", g=NG)
                tt(ch8, ch8, GMK[:, 0:nt].unsqueeze(3).broadcast_to((P, nt, NG, 8)), ALU.add).then_inc(*done('DVE', 'rt.masked', l))
                wait('DVE', 'rt.masked', l)
                for i in range(nt):
                    last = dve.max(E8[:, i, :], CH[:, i, :])
                last.then_inc(*done('DVE', 'rt.etop', l))
                wait('DVE', 'rt.etop', l)
                for i in range(nt):
                    last = dve.max_index(EIX[:, i, :].bitcast(mybir.dt.uint32), E8[:, i, :], CH[:, i, :])
                last.then_inc(*done('DVE', 'rt.eidx', l))
                wait('DVE', 'rt.eidx', l)
                dve.tensor_copy(EIF[:, 0:nt], EIX[:, 0:nt]).then_inc(*done('DVE', 'rt.efloat', l))
                wait('DVE', 'rt.efloat', l)
                for i in range(nt):
                    last = tt(OH[:, 6 * i:6 * i + 6, :], bcast(EIF[:, i, 0:TOPK], P, TOPK, NE),
                              C('experts').unsqueeze(1).broadcast_to((P, TOPK, NE)), ALU.is_equal)
                last.then_inc(*done('DVE', 'rt.ehot', l))
                wait('DVE', 'rt.ehot', l)
                tt(OH2[:, 0:6 * nt], OH[:, 0:6 * nt], bcast(C('codes')[:, 0:6 * nt], P, 6 * nt, NE)).then_inc(*done('DVE', 'rt.coded', l))
                wait('DVE', 'rt.coded', l)
                for i in range(nt):
                    last = dve.tensor_reduce(VC[:, i, :], OH2[:, 6 * i:6 * i + 6, :].rearrange("p k e -> p e k"), AX.X, ALU.add)
                last.then_inc(*done('DVE', 'rt.vc', l))
                wait('DVE', 'rt.vc', l)
                for i in range(nt):
                    last = tt(OH2[:, 6 * i:6 * i + 6, :], OH[:, 6 * i:6 * i + 6, :], LG[:, i, :].unsqueeze(1).broadcast_to((P, TOPK, NE)))
                last.then_inc(*done('DVE', 'rt.wprod', l))
                wait('DVE', 'rt.wprod', l)
                dve.tensor_reduce(WK[:, 0:nt].rearrange("p i k -> p (i k)"), OH2[:, 0:6 * nt], AX.X, ALU.add).then_inc(*done('DVE', 'rt.w', l))
                wait('DVE', 'rt.w', l)
                dve.tensor_reduce(WS[:, 0:nt], WK[:, 0:nt], AX.X, ALU.add).then_inc(*done('DVE', 'rt.wsum', l))
                wait('DVE', 'rt.wsum', l)
                dve.reciprocal(WS[:, 0:nt], WS[:, 0:nt]).then_inc(*done('DVE', 'rt.winv', l))
                wait('DVE', 'rt.winv', l)
                stt(WK[:, 0:nt], WK[:, 0:nt], 2.5, bcast(WS[:, 0:nt], P, nt, TOPK)).then_inc(*done('DVE', 'rt.wts', l))

                wait('PE', 'rt.vt', l)
                dve.tensor_copy(VT[:, 0:n_tok], bank[1][0:NE, 0:n_tok]).then_inc(*done('DVE', 'rt.vtout', l))
                wait('DVE', 'rt.vtout', l)
                for f in range(2):
                    wait('ACT', 'sh.silu', l, f)
                    wait('PE', 'sh.up', l, f, 1)
                    tt(SH2[:, f, 0:n_tok], SH1[:, f, 0:n_tok], bank[5 + 2 * f][:, 0:n_tok]).then_inc(*done('DVE', 'sh.act', l, f))
                for r in range(CAP // 8):
                    if r > 0:
                        wait('DVE', 'rt.drop', l, r - 1)
                    dve.max(LST[:, 8 * r:8 * r + 8], VT[:, 0:n_tok]).then_inc(*done('DVE', 'rt.list', l, r))
                    wait('DVE', 'rt.list', l, r)
                    dve.match_replace(VT[:, 0:n_tok], LST[:, 8 * r:8 * r + 8], VT[:, 0:n_tok], 0.0).then_inc(*done('DVE', 'rt.drop', l, r))
                wait('DVE', 'rt.drop', l, CAP // 8 - 1)
                dve.tensor_reduce(LEFT[0:NE], VT[:, 0:n_tok], AX.X, ALU.max).then_inc(*done('DVE', 'rt.left', l))
                for m in range(KD):
                    wait('PE', 'sh.down', l, m)
                    for g in reversed(streams):
                        q = slice(SEQ * g, SEQ * g + SEQ)
                        stt(xT[:, m, q], bank[2 + m % 2][:, q], md[:, 40 + m, g:g + 1], xT[:, m, q], ALU.mult, ALU.add
                            ).then_inc(*done('DVE', 'sh.x', l, m, g))

                wait('PE', 'rt.slots', l)
                dve.tensor_copy(flags[:, l:l + 1], bank[1][:, NE:NE + 1]).then_inc(*done('DVE', 'rt.flag', l))
                dve.tensor_scalar(CODI[:, 0:NE], bank[1][:, 0:NE], -1.0, float(CODES), ALU.mult, ALU.add).then_inc(*done('DVE', 'rt.code', l))
                wait('DVE', 'rt.code', l)
                dve.tensor_scalar(TOKI[:, 0:NE], CODI[:, 0:NE], 3, None, ALU.logical_shift_right).then_inc(*done('DVE', 'rt.tok', l))

                def rows_half(e, r):
                    dve.wait_ge(m_sem(l, 'xg_turned'), e + 1)
                    dve.tensor_copy(xgT[:, r, 0:512], bank[0][:]).then_inc(m_sem(l, 'xgT_dve'), 1)

                def inner(e, r):
                    dve.wait_ge(m_sem(l, 'silu_done'), e + 1)
                    tt(hh[:, r, :], sg[:, r, :], bank[2][:, FF:2 * FF]).then_inc(m_sem(l, 'inner_done'), 1)

                def out_half(e, r, sent):
                    dve.wait_ge(st.sem(f'expert_done{l}'), e + 1)
                    if not (isinstance(sent, int) and sent == 0):
                        dve.wait_ge(m_sem(l, f'yy_sent{r}'), sent)
                    dve.tensor_copy(yy[:, r, 0:512], bank[4][:]).then_inc(m_sem(l, 'yy_dve'), 1)

                moe_walk(dve, inner, rows_half, out_half, lambda e, r: None)

                wait('DVE', 'rt.flag', l)
                more = n_tok // CAP - 1
                with dve.If(dve.value_load(flags[0:1, l:l + 1], min_val=0, max_val=NE * CODES) > 0):
                    for r in range(more * CAP // 8):
                        codes = LST[:, CAP + 8 * r:CAP + 8 * r + 8]
                        if r > 0:
                            dve.wait_ge(m_sem(l, 'more_dropped'), r)
                        dve.max(codes, VT[:, 0:n_tok]).then_inc(m_sem(l, 'more_listed'), 1)
                        dve.wait_ge(m_sem(l, 'more_listed'), r + 1)
                        dve.match_replace(VT[:, 0:n_tok], codes, VT[:, 0:n_tok], 0.0).then_inc(m_sem(l, 'more_dropped'), 1)
                    dve.wait_ge(m_sem(l, 'more_turned'), 1)
                    for k in range(more):
                        last = dve.tensor_scalar(CODI[:, NE + k:NE + NE * more:more], bank[6][:, NE * k:NE * k + NE], -1.0, float(CODES),
                                                 ALU.mult, ALU.add)
                    last.then_inc(m_sem(l, 'more_codes'), 1)
                    dve.wait_ge(m_sem(l, 'more_codes'), 1)
                    dve.tensor_scalar(TOKI[:, NE:NE + NE * more], CODI[:, NE:NE + NE * more], 3, None, ALU.logical_shift_right
                                      ).then_inc(m_sem(l, 'more_codes'), 1)
                    with dve.Fori(0, NE * more) as q:
                        rows_half(NE + q, 0)
                        inner(NE + q, 0)
                        out_half(NE + q, 0, 16 * q + 16 * IN_SLOT0)

                for i in range(nt):
                    wait('DMA', 'comb.rows', l, i)
                    if i >= 1:
                        wait('PE', 'comb.turn', l, i - 1)
                    for k in range(TOPK):
                        if k == 0:
                            last = dve.tensor_scalar(YC, YR[:, 0, :], WK[:, i, 0:1], None, ALU.mult)
                        else:
                            wait('DVE', 'comb.sum', l, i, k - 1)
                            last = stt(YC, YR[:, k, :], WK[:, i, k:k + 1], YC, ALU.mult, ALU.add)
                        last.then_inc(*done('DVE', 'comb.sum', l, i, k))
                    wait('PE', 'comb.turn', l, i)
                    q, g = slice(P * i, P * i + P), i // NLAT
                    for c in range(KD):
                        stt(xT[:, c, q], bank[6 + c // 4][:, P * (c % 4):P * (c % 4) + P], md[:, 40 + c, g:g + 1], xT[:, c, q], ALU.mult, ALU.add
                            ).then_inc(*done('DVE', 'comb.x', l, i, c))

            inverse_root(0, 'fin', SEQ)
            for c in range(KD):
                stt(hT[:, c, 0:SEQ], xT[:, c, 0:SEQ], cols[0][:, 64 + c:65 + c], rstd2_t[:, 0:SEQ]).then_inc(*done('DVE', 'fin.scale', 0, c))
            for i in range(NLAT):
                wait('PE', 'fin.turn', 0, i, 0)
                dve.tensor_copy(HR[:, i, 0:512], bank[2 * i][:]).then_inc(*done('DVE', 'fin.rows', 0, i, 0))

        @block.scalar
        def _(act):
            def wait(*step):
                act.wait_ge(*after(*step))

            def copy_out(dst, src, factor=1.0):
                return act.activation(dst, src, ACT.Copy, scale=factor)

            def func(o, a, f, **kw):
                return act.activation(o, a, f, **kw)

            eps, one = C('eps'), C('ones')[:, 0:1]

            def squares(l, norm, n):
                for c in range(KD):
                    func(hT[:, c, 0:n], xT[:, c, 0:n], ACT.Square).then_inc(*done('ACT', norm + '.sq', l, c))

            def root(l, norm, n, dst):
                wait('PE', norm + '.sum', l)
                func(dst[:, 0:n], bank[6][:, 0:n], ACT.Sqrt, bias=eps, scale=1.0 / D).then_inc(*done('ACT', norm + '.root', l))

            wait('DVE', 'start.cols', 0, 0)
            func(SC, cols[0][:, 72:88].rearrange("p (g k) -> p k g", g=2), ACT.Silu).then_inc(*done('ACT', 'start.sc', 0))
            for c in range(0, KD, 2):
                wait('PE', 'start.x', 0, c)
                copy_out(xT[:, c], bank[(c + 1) % 8][:]).then_inc(*done('ACT', 'start.x', 0, c))

            for l in range(DEPTH):
                n_tok, nt = P * tiles(l), tiles(l)
                streams = range(2) if not latent(l) else range(1)
                md = mod[l][:].rearrange("p (m g) -> p m g", g=2)
                b = bc[l]

                if l == 0:
                    wait('DVE', 'start.x', 0, 7)
                    wait('ACT', 'start.x', 0, 6)
                else:
                    wait('DVE', 'comb.x', l - 1, NT - 1, KD - 1)
                squares(l, 'norm1', T)
                root(l, 'norm1', T, rstd_s)
                wait('DVE', 'lam.sum', l)
                func(lamt[:, 2:4], lamt[:, 0:2], ACT.Exp).then_inc(*done('ACT', 'lam.exp', l))
                func(NEXP, b[:, 644:652], ACT.Exp).then_inc(*done('ACT', 'lam.alog', l))
                for c in range(KD):
                    for g in range(2):
                        wait('DVE', 'norm1.scale', l, c, g)
                        q = slice(SEQ * g, SEQ * g + SEQ)
                        last = func(hT[:, c, q], hT[:, c, q], ACT.Identity, bias=md[:, c, g:g + 1])
                    last.then_inc(*done('ACT', 'norm1.bias', l, c))

                wait('Pool', 'pad.zero', l)
                wait('DVE', 'norm1.scale', l, KD - 1, 1)
                for u in range(NT * len(PIECES) + 6):
                    if evac_engine(u) != 'ACT':
                        continue
                    if u < NT * len(PIECES):
                        pi, i = divmod(u, NT)
                        wait('PE', 'proj.unit', l, pi, i)
                        for dst, to, at_, n in PIECES[pi][3]:
                            last = copy_out(*piece_views(dst, to, bank[u % 4], at_, n, i))
                    else:
                        m = u - NT * len(PIECES)
                        wait('PE', 'proj.dqkv', l, m)
                        last = copy_out(GP[:, m].rearrange("p (g n) -> p g n", g=2)[:, :, 2:258],
                                        bank[u % 4][:].rearrange("p (g n) -> p g n", g=2))
                    last.then_inc(*done('ACT', 'proj.out', l, u))
                wait('DVE', 'proj.out', l, 19)
                wait('ACT', 'proj.out', l, 18)
                for i in range(NT):
                    for q, (a_, n_) in enumerate(((0, 192), (192, 128))):
                        if i or q:
                            wait('ACT', 'lat.sq', l, i if q else i - 1, 1 - q)
                        func(SM[:, 0:n_], CC[:, i, a_:a_ + n_], ACT.Square, accum_out=SST[:, i, q:q + 1]).then_inc(*done('ACT', 'lat.sq', l, i, q))
                wait('ACT', 'lat.sq', l, NT - 1, 1)
                func(SST[:, :, 2], SST[:, :, 0], ACT.Sqrt, bias=eps, scale=1.0 / 192)
                func(SST[:, :, 3], SST[:, :, 1], ACT.Sqrt, bias=eps, scale=1.0 / 128).then_inc(*done('ACT', 'lat.root', l))
                for k in range(0, len(TR), 2):
                    _, dst, r, f = TR[k]
                    wait('PE', 'tr.unit', l, k)
                    if k == 0:
                        wait('DVE', 'rope.k.sum', l)
                    copy_out(dst[0:r], bank[(k + 4) % 8][0:r, :], f).then_inc(*done('ACT', 'tr.out', l, k))
                for v in range(0, 8, 2):
                    wait('PE', 'up.unit', l, v)
                    o = bank[(6 + v) % 8]
                    (copy_out(QM[:, v, :], o[:, 0:384]) if v < 4 else copy_out(KV[:, v - 4, :], o[:])
                     ).then_inc(*done('ACT', 'up.out', l, v))
                for k in range(0, len(TM), 2):
                    _, dst, r, f = TM[k]
                    wait('PE', 'tm.unit', l, k)
                    if k == 0:
                        wait('Pool', 'kf.rope', l)
                    copy_out(dst[0:r], bank[(6 + k) % 8][0:r, :], f).then_inc(*done('ACT', 'tm.out', l, k))

                U = 16 * nt
                wait('Pool', 'kf.rope', l)
                for step in range(U + 4):
                    u = step
                    if u < U:
                        i, m = divmod(u, 16)
                        n = P * len(key_tiles(i))
                        wait('DVE', 'att.max', l, u)
                        if u >= 3:
                            wait('PE', 'att.pt', l, u - 3)
                        elif u == 0:
                            wait('PE', 'tm.unit', l, 7)
                        src = SM[:, 0:n] if m < 4 and i < NLAT else bank[u % 2][:, 0:n]
                        func(PX[:, u % 3, 0:n], src, ACT.Exp, bias=NEGM[:, i, m:m + 1], accum_out=SUMS[:, i, m:m + 1]
                             ).then_inc(*done('ACT', 'att.exp', l, u))
                    u = step - 1
                    if 0 <= u < U and evac_engine(u) == 'ACT':
                        i, m = divmod(u, 16)
                        n = P * len(key_tiles(i))
                        wait('PE', 'att.pt', l, u)
                        if u >= 3:
                            wait('PE', 'att.pv', l, u - 3)
                        copy_out(PXT[:, u % 3, 0:n], bank[2 + u % 2][:, 0:n]).then_inc(*done('ACT', 'att.pt', l, u))
                    if step >= 19 and (step - 19) % 16 == 0:
                        i = (step - 19) // 16
                        wait('DVE', 'att.sink', l, i)
                        func(ESINK[:, i, :], ESINK[:, i, :], ACT.Exp).then_inc(*done('ACT', 'att.sink', l, i))
                wait('DVE', 'att.dif', l, nt - 1)
                func(DSQ[:, 0:4 * nt, :].rearrange("p (i h) n -> p i (h n)", h=4), Y[:, 0:nt, 256:512], ACT.Square).then_inc(*done('ACT', 'dif.sq', l))
                ga, gb = DZ[:, :, 256:264], DZ[:, :, 264:272]
                wait('DVE', 'dif.ss', l)
                func(GNS[:, 0:4 * nt], GNS[:, 0:4 * nt], ACT.Sqrt, bias=eps, scale=1.0 / 64).then_inc(*done('ACT', 'dif.root', l))
                wait('DVE', 'att.y', l, nt - 1, 1)
                func(GB, gb, ACT.Exp, scale=-1.0).then_inc(*done('ACT', 'gate.beta', l))
                wait('DVE', 'gate.min', l)
                func(GG, GN, ACT.Exp).then_inc(*done('ACT', 'gate.exp', l))
                wait('ACT', 'gate.exp', l)
                func(GG, GG, ACT.Ln, bias=one).then_inc(*done('ACT', 'gate.ln', l))
                for c in range(6):
                    wait('DVE', 'conv.tap', l, 4, c)
                    func(CV[:, c], CV[:, c], ACT.Silu).then_inc(*done('ACT', 'conv.silu', l, c))
                for n in range(0, 8, 2):
                    wait('PE', 'gt.unit', l, n)
                    copy_out(GT[:, n // 2, 0:512], bank[n][:]).then_inc(*done('ACT', 'gt.out', l, n))
                wait('ACT', 'gt.out', l, 6)
                func(QSQ.rearrange("p (i h) n -> p i (h n)", h=8), GT[:, :, 0:512], ACT.Square).then_inc(*done('ACT', 'qk.sq', l))
                wait('DVE', 'qk.ss', l)
                func(GW, GW, ACT.Sqrt, bias=eps).then_inc(*done('ACT', 'qk.root', l))
                for n in range(0, 8, 2):
                    wait('PE', 'gq.unit', l, n)
                    copy_out(GQ[:, n // 2, :], bank[n][0:64, :]).then_inc(*done('ACT', 'gq.out', l, n))

                for s in range(4):
                    for name in ACT_SCAN:
                        for d in range(2):
                            i, w = scan_tile(s, d), W[d]
                            if name in ('attt', 'qgt', 'o') and skip_scan(l, s, d, name) or name == 'o' and s % 2:
                                continue
                            o = lambda x: bank[scan_bank(x, d)]
                            last_column = P - 1 if d == 0 else 0
                            if name == 'eg':
                                wait('DVE', 'gc.out', l)
                                if s > 0:
                                    wait('Pool', 'scan.kdec', l, s - 1, d)
                                last = func(w['eg'], GC[:, i, 4 * d:4 * d + 4], ACT.Exp)
                            elif name == 'egl':
                                wait('DVE', 'scan.dd', l, s, d)
                                if s > 1:
                                    wait('DVE', 'scan.sdec', l, s - 1, d)
                                last = func(w['egl'], o('rb')[:].rearrange("p (h n) -> p h n", h=4)[:, :, last_column], ACT.Exp)
                            elif name == 'ekd':
                                wait('DVE', 'scan.dd', l, s, d)
                                last = func(w['ekd'], w['att'].rearrange("p (h n) -> p h n", h=4)[:, :, last_column], ACT.Exp)
                            elif name == 'dec':
                                wait('DVE', 'scan.big', l, s, d)
                                last = func(w['dec'], w['dec'], ACT.Exp, scale=-1.0)
                            elif name in ('wt', 'qgt'):
                                wait('PE', 'scan.' + name, l, s, d)
                                last = copy_out(w[name][0:64], o(name)[0:64, :])
                            elif name == 'o':
                                wait('PE', 'scan.o', l, s, d)
                                last = copy_out(Y[:, i, 768:1024], o('o')[:, 0:256])
                            else:
                                wait('PE', 'scan.' + name, l, s, d)
                                last = copy_out(w[name], o(name)[:])
                            last.then_inc(*done('ACT', 'scan.' + name, l, s, d))
                for i in range(nt):
                    d = [d for d in range(2) if not skip_scan(l, first_visit(i, 1 - d)[0], d, 'o') and first_visit(i, 1 - d)[0] % 2][0]
                    wait('DVE', 'scan.o', l, first_visit(i, 1 - d)[0], d)
                for d in range(2):
                    wait('DVE', 'scan.u', l, 3, d)
                func(GSQ[:, 0:4 * nt, :].rearrange("p (i h) n -> p i (h n)", h=4), Y[:, 0:nt, 768:1024], ACT.Square).then_inc(*done('ACT', 'gout.sq', l))
                func(DZ[:, 0:nt, 0:256], DZ[:, 0:nt, 0:256], ACT.Silu).then_inc(*done('ACT', 'gout.z', l))
                wait('DVE', 'gout.ss', l)
                func(GNS[:, 0:4 * nt], GNS[:, 0:4 * nt], ACT.Sqrt, bias=eps, scale=1.0 / 64).then_inc(*done('ACT', 'gout.root', l))

                for c in range(0, KD, 2):
                    wait('PE', 'yt.unit', l, c)
                    copy_out(YT[:, c, 0:n_tok], bank[c % 4][:, 0:n_tok]).then_inc(*done('ACT', 'yt.out', l, c))
                for c in range(KD):
                    wait('DVE', 'out.x', l, c, 0)
                    func(hT[:, c, 0:n_tok], xT[:, c, 0:n_tok], ACT.Square).then_inc(*done('ACT', 'norm2.sq', l, c))
                root(l, 'norm2', n_tok, rstd2_s)
                for c in range(KD):
                    for g in streams:
                        wait('DVE', 'norm2.scale', l, c, g)
                        q = slice(SEQ * g, SEQ * g + SEQ)
                        last = func(hT[:, c, q], hT[:, c, q], ACT.Identity, bias=md[:, 24 + c, g:g + 1])
                    last.then_inc(*done('ACT', 'norm2.bias', l, c))
                wait('PE', 'rt.logits', l, nt - 1)
                func(LG[:, 0:nt], bank[0][:, 0:NE * nt].rearrange("p (i e) -> p i e", e=NE), ACT.Sigmoid).then_inc(*done('ACT', 'rt.sig', l))
                for i in range(nt):
                    wait('PE', 'rt.rows', l, i, 1)
                    if i >= 2:
                        wait('DMA', f'h2row{i % 2}.out', l, i - 2)
                    copy_out(HR[:, i % 2, 512:1024], bank[3][:]).then_inc(*done('ACT', 'rt.rows', l, i, 1))
                    wait('ACT', 'rt.rows', l, i, 1)
                    wait('DVE', 'rt.rows', l, i, 0)
                    act.dma_start(h2_rows[P * i:P * i + P, :], HR[:, i % 2, :]).then_inc(*done('DMA', f'h2row{i % 2}.out', l, i, by=16))
                for f in range(2):
                    wait('PE', 'sh.up', l, f, 0)
                    if f == 0:
                        wait('DMA', 'h2row0.out', l, nt - 2)
                        wait('DMA', 'h2row1.out', l, nt - 1)
                    func(SH1[:, f, 0:n_tok], bank[4 + 2 * f][:, 0:n_tok], ACT.Silu).then_inc(*done('ACT', 'sh.silu', l, f))

                def rows_half(e, r):
                    act.wait_ge(m_sem(l, 'xg_turned'), e + 1)
                    copy_out(xgT[:, r, 512:1024], bank[1][:]).then_inc(m_sem(l, 'xgT_act'), 1)

                def gate(e, r):
                    act.wait_ge(m_sem(l, 'up_done'), e + 1)
                    func(sg[:, r, :], bank[2][:, 0:FF], ACT.Silu).then_inc(m_sem(l, 'silu_done'), 1)

                def out_half(e, r, sent):
                    act.wait_ge(st.sem(f'expert_done{l}'), e + 1)
                    if not (isinstance(sent, int) and sent == 0):
                        act.wait_ge(m_sem(l, f'yy_sent{r}'), sent)
                    copy_out(yy[:, r, 512:1024], bank[5][:]).then_inc(m_sem(l, 'yy_act'), 1)

                def inner_rows(e, r):
                    act.wait_ge(m_sem(l, 'inner_turned'), e + 1)
                    copy_out(hhT[:, r, :], bank[3][:, 0:FF]).then_inc(m_sem(l, 'hhT_done'), 1)

                moe_walk(act, gate, rows_half, out_half, inner_rows)

                wait('DVE', 'rt.flag', l)
                more = n_tok // CAP - 1
                with act.If(act.value_load(flags[0:1, l:l + 1], min_val=0, max_val=NE * CODES) > 0):
                    with act.Fori(0, NE * more) as q:
                        rows_half(NE + q, 0)
                        gate(NE + q, 0)
                        inner_rows(NE + q, 0)
                        out_half(NE + q, 0, 16 * q + 16 * IN_SLOT0)
                    act.wait_ge(m_sem(l, 'yy_sent0'), 16 * (IN_SLOT0 + NE * more))

                y_k = y_rows.rearrange("(t e) n -> t e n", e=8)
                for i in range(nt):
                    if i == 0:
                        for r in range(RING):
                            act.wait_ge(m_sem(l, f'yy_sent{r}'), 16 * len(range(r, NE, RING)))
                    else:
                        wait('DVE', 'comb.sum', l, i - 1, TOPK - 1)
                    act.dma_start(YR, y_k[P * i:P * i + P, 0:TOPK, :]).then_inc(*done('DMA', 'comb.rows', l, i, by=16))

            wait('DVE', 'comb.x', DEPTH - 1, NLAT - 1, KD - 1)
            squares(0, 'fin', SEQ)
            root(0, 'fin', SEQ, rstd2_s)
            for i in range(NLAT):
                wait('PE', 'fin.turn', 0, i, 1)
                copy_out(HR[:, i, 512:1024], bank[2 * i + 1][:]).then_inc(*done('ACT', 'fin.rows', 0, i, 1))
                wait('ACT', 'fin.rows', 0, i, 1)
                wait('DVE', 'fin.rows', 0, i, 0)
                act.dma_start(out[0, P * i:P * i + P, :], HR[:, i, :]).then_inc(*done('DMA', 'result.out', 0, i, by=16))
            wait('DMA', 'result.out', 0, NLAT - 1)

        @block.gpsimd
        def _(pool):
            def wait(*step):
                pool.wait_ge(*after(*step))

            def tt(o, a, b, op=ALU.mult):
                return pool.tensor_tensor(o, a, b, op)

            for l in range(DEPTH):
                n_tok = P * tiles(l)
                if l > 0:
                    wait('DVE', 'comb.x', l - 1, NT - 1, KD - 1)
                pool.memset(GP, 0.0).then_inc(*done('Pool', 'pad.zero', l))
                for v in range(4, 8):
                    wait(evac_engine(v), 'up.out', l, v)
                wait('DVE', 'rope.k.sum', l)
                kf = KF.rearrange("p (i h) n -> p i h n", h=4)
                pool.tensor_copy(KF[:, :, 0:64], KV.rearrange("p i (h n) -> p (i h) n", n=128)[:, :, 0:64]).then_inc(*done('Pool', 'kf.own', l))
                pool.tensor_copy(kf[:, :, :, 64:96], CC[:, :, 320:352].unsqueeze(2).broadcast_to((P, NT, 4, 32))
                                 ).then_inc(*done('Pool', 'kf.rope', l))

                wait('DVE', 'gc.out', l)
                wait('DVE', 'qk.norm', l)
                wait('DVE', 'gate.nb', l)
                heads = lambda v: v.rearrange("p (h n) -> p h n", h=4)
                for s in range(4):
                    for name in POOL_SCAN:
                        for d in range(2):
                            i, w = scan_tile(s, d), W[d]
                            step = ('Pool', 'scan.' + name, l, s, d)
                            four = lambda v: v.unsqueeze(2).broadcast_to((P, 4, 64))
                            q = GT[:, i, 0:256].rearrange("p (h n) -> p h n", h=4)
                            k = GT[:, i, 256:512].rearrange("p (h n) -> p h n", h=4)
                            v = GT[:, i, 512:768].rearrange("p (h n) -> p h n", h=4)
                            r = w['r'].rearrange("p (h n) -> p h n", h=4)
                            if name == 'cum':
                                if s > 0:
                                    wait('PE', 'scan.z3', l, s - 1, d)
                                last = tt(heads(w['cum']), C('le' if d == 0 else 'ge').unsqueeze(1).broadcast_to((P, 4, P)),
                                          GG[:, i, 4 * d:4 * d + 4].unsqueeze(2).broadcast_to((P, 4, P)))
                            elif name == 'beg':
                                wait('ACT', 'scan.eg', l, s, d)
                                last = tt(w['beg'], GB[:, i, 4 * d:4 * d + 4], w['eg'])
                            elif name == 'rv':
                                if s > 0:
                                    wait(*(('PE', 'scan.ws') if s > 1 else ('ACT', 'scan.wt')), l, s - 1, d)
                                last = tt(r[:, :, 0:64], v, four(GB[:, i, 4 * d:4 * d + 4]))
                            elif name == 'rk':
                                wait('Pool', 'scan.beg', l, s, d)
                                last = tt(r[:, :, 64:128], k, four(w['beg']))
                            elif name == 'n':
                                wait('DVE', 'scan.kb', l, s, d)
                                if s > 0:
                                    wait('PE', 'scan.mt', l, s - 1, d)
                                last = tt(heads(w['n']), heads(w['kd']), C('off_f' if d == 0 else 'off_b').unsqueeze(1).broadcast_to((P, 4, P)))
                            elif name == 'qg':
                                if s > 0 and not skip_scan(l, s - 1, d, 'qgt'):
                                    wait('PE', 'scan.qgt', l, s - 1, d)
                                last = tt(w['qg'].rearrange("p (h n) -> p h n", h=4), q, four(w['eg']))
                            elif name == 'kdec':
                                if s == 3:
                                    continue
                                wait('ACT', 'scan.ekd', l, s, d)
                                if s > 0:
                                    wait('PE', 'scan.sn', l, s - 1, d)
                                last = tt(w['kdec'].rearrange("p (h n) -> p h n", h=4), k, four(w['ekd']))
                            last.then_inc(*done(*step))

                wait('DVE', 'rt.tok', l)
                wait('DMA', 'h2row0.out', l, tiles(l) - 2)
                wait('DMA', 'h2row1.out', l, tiles(l) - 1)
                wait('DVE', 'sh.act', l, 1)
                pool.memset(xg, 0.0).then_inc(*done('Pool', 'xg.zero', l))
                wait('Pool', 'xg.zero', l)

                last_token, last_code = pool.to_reg(n_tok - 1), pool.to_reg(CODES - 1)

                def gather(e, r, turned):
                    if not (isinstance(turned, int) and turned == 0):
                        pool.wait_ge(m_sem(l, 'xg_turned'), turned)
                    column = bass.ds(e, 1) if not isinstance(e, int) else slice(e, e + 1)
                    pool.tensor_copy(tix[:, r:r + 1], TOKI[:, column])
                    pool.drain()
                    pool.indirect_dma_start(xg[:, r, :], None, h2_rows, bass.IndirectOffsetOnAxis(ap=tix[:, r:r + 1], axis=0),
                                            bounds_check=last_token, oob_is_err=False).then_inc(m_sem(l, f'xg_loaded{r}'), 16)

                def scatter(e, r, sent):
                    pool.wait_ge(m_sem(l, 'yy_dve'), e + 1)
                    pool.wait_ge(m_sem(l, 'yy_act'), e + 1)
                    if not (isinstance(sent, int) and sent == 0):
                        pool.wait_ge(m_sem(l, f'yy_sent{r}'), sent)
                    column = bass.ds(e, 1) if not isinstance(e, int) else slice(e, e + 1)
                    pool.tensor_copy(cix[:, r:r + 1], CODI[:, column])
                    pool.drain()
                    pool.indirect_dma_start(y_rows, bass.IndirectOffsetOnAxis(ap=cix[:, r:r + 1], axis=0), yy[:, r, :], None,
                                            bounds_check=last_code, oob_is_err=False).then_inc(m_sem(l, f'yy_sent{r}'), 16)

                for e in range(RING):
                    gather(e, e, 0)

                def three(j):
                    for u in range(RING):
                        gather(RING * j + (RING + u), u, RING * j + (u + 1))
                        scatter(RING * j + u, u, 16 * j)

                three(0)
                with pool.Fori(1, (NE - RING) // RING) as j:
                    three(j)
                for e in range(RING * ((NE - RING) // RING), NE):
                    if e + RING < NE:
                        gather(e + RING, e % RING, e + 1)
                    scatter(e, e % RING, 16 * (e // RING))

                more = n_tok // CAP - 1
                wait('DVE', 'rt.flag', l)
                with pool.If(pool.value_load(flags[0:1, l:l + 1], min_val=0, max_val=NE * CODES) > 0):
                    pool.wait_ge(m_sem(l, 'more_codes'), 2)
                    with pool.Fori(0, NE * more) as q:
                        gather(NE + q, 0, NE + q)
                        scatter(NE + q, 0, 16 * q + 16 * IN_SLOT0)

        return st.seen


NAMES = ('x', 'c', 'ctx', 'c_ctx', 'w_ada', 'b_ada', 'norm1_g', 'norm2_g', 'w_in', 'w_out', 'swa_sinks', 'diff_lq1', 'diff_lk1',
         'diff_lq2', 'diff_lk2', 'diff_norm_g', 'mla_q_norm_g', 'mla_kv_norm_g', 'mla_w_uq', 'mla_w_ukv', 'gdn_conv_w',
         'gdn_a_log_f', 'gdn_a_log_b', 'gdn_dt_bias_f', 'gdn_dt_bias_b', 'gdn_norm_g', 'moe_w_router', 'moe_bias', 'moe_w_gate',
         'moe_w_up', 'moe_w_down', 'shared_w_gate', 'shared_w_up', 'shared_w_down', 'final_norm_g')


def program(nc, arrays, known):
    io = {n: nc.dram_tensor('in_' + n, a.shape, F32, kind="ExternalInput").ap() for n, a in arrays.items()}
    out = nc.dram_tensor('out_0', (1, SEQ, D), F32, kind="ExternalOutput").ap()
    return build(nc, io, out, known)


def kernel(**inputs):
    import concourse.bacc as _bacc
    from concourse.bass_utils import run_bass_kernel_spmd as _run

    arrays = {n: np.ascontiguousarray(inputs[n]) for n in NAMES}
    arrays['cst'] = constants()
    known = program(_bacc.Bacc("TRN2", target_bir_lowering=False, num_devices=1), arrays, None)
    nc = _bacc.Bacc("TRN2", target_bir_lowering=False, num_devices=1)
    program(nc, arrays, known)
    r = _run(nc, [{'in_' + n: a for n, a in arrays.items()}], core_ids=[0])
    return r.results[0]['out_0']
```
